# Optimizing a Trainium2 kernel written in Bass

```python
import math
import jax, jax.numpy as jnp
from jax import lax
import numpy as np

D_MODEL = 1024
BATCH = 1
SEQ = 512
DEPTH = 2

N_EVEN = (DEPTH + 1) // 2
N_ODD = DEPTH // 2

ALPHA = (2 * DEPTH) ** 0.25
BETA = (8 * DEPTH) ** -0.25
LN_EPS = 1e-5

MLSTM_HEADS = 4
RET_HEADS = 4
HEAD_DIM = D_MODEL // 8
MLSTM_W = MLSTM_HEADS * HEAD_DIM
RET_W = RET_HEADS * HEAD_DIM
CHUNK = 128
CONV_WIDTH = 4
IN0_SPLITS = (MLSTM_W, 2 * MLSTM_W, 3 * MLSTM_W, 4 * MLSTM_W,
              4 * MLSTM_W + MLSTM_HEADS, 4 * MLSTM_W + 2 * MLSTM_HEADS,
              4 * MLSTM_W + 2 * MLSTM_HEADS + RET_W,
              4 * MLSTM_W + 2 * MLSTM_HEADS + 2 * RET_W,
              4 * MLSTM_W + 2 * MLSTM_HEADS + 3 * RET_W)
IN0_COLS = 4 * MLSTM_W + 2 * MLSTM_HEADS + 4 * RET_W

DIL_HEADS = 8
DIL_DH = D_MODEL // 16
DIL_W = DIL_HEADS * DIL_DH
DIL_CONFIGS = ((128, 1), (512, 4), (2048, 16))
IN1_COLS = len(DIL_CONFIGS) * 3 * DIL_W

N_EXPERTS = 32
N_GROUPS = 4
EXPERTS_PER_GROUP = N_EXPERTS // N_GROUPS
TOP_K = 2
D_EXPERT = D_MODEL // 4
MOE_BLOCK = 128

kernel_name = "hybrid_mlstm_retention_dilated_moe_deepnorm"

def layer_norm(x, g, b):
    xf = x.astype(jnp.float32)
    mu = jnp.mean(xf, -1, keepdims=True)
    var = jnp.mean(jnp.square(xf - mu), -1, keepdims=True)
    return ((xf - mu) * lax.rsqrt(var + LN_EPS)).astype(x.dtype) * g + b

def head_norm(h, g):
    B, T, H, dh = h.shape
    mu = jnp.mean(h, -1, keepdims=True)
    var = jnp.mean(jnp.square(h - mu), -1, keepdims=True)
    y = (h - mu) * lax.rsqrt(var + LN_EPS)
    return y.reshape(B, T, H * dh) * g.astype(jnp.float32)

def causal_depthwise_conv(x, w, b):
    K, C = w.shape
    y = lax.conv_general_dilated(x, w[:, None, :], window_strides=(1,),
                                 padding=[(K - 1, 0)],
                                 dimension_numbers=('NWC', 'WIO', 'NWC'),
                                 feature_group_count=C)
    return y + b

def to_chunks(a):
    n = a.shape[2] // CHUNK
    a = a.reshape(a.shape[:2] + (n, CHUNK) + a.shape[3:])
    return jnp.moveaxis(a, 2, 0)

def from_chunks(a):
    a = jnp.moveaxis(a, 0, 2)
    return a.reshape(a.shape[:2] + (a.shape[2] * a.shape[3],) + a.shape[4:])

def mlstm_chunkwise(q, k, v, i_pre, log_f):
    B, H, T, dh = q.shape
    causal = jnp.tril(jnp.ones((CHUNK, CHUNK), bool))

    def step(carry, inp):
        C, n, m = carry
        qb, kb, vb, ib, fb = inp
        b = jnp.cumsum(fb, axis=-1)
        g = b[..., -1]
        log_d = jnp.where(causal, b[..., :, None] - b[..., None, :] + ib[..., None, :], -jnp.inf)
        a = b + m[..., None]
        m_t = jnp.maximum(a, jnp.max(log_d, -1))
        d = jnp.exp(log_d - m_t[..., None])
        inter = jnp.exp(a - m_t)
        s = jnp.einsum('bhld,bhsd->bhls', qb, kb) * d
        num = jnp.einsum('bhls,bhse->bhle', s, vb) + inter[..., None] * jnp.einsum('bhld,bhde->bhle', qb, C)
        den = jnp.sum(s, -1) + inter * jnp.einsum('bhld,bhd->bhl', qb, n)
        h = num / jnp.maximum(jnp.abs(den), jnp.exp(-m_t))[..., None]
        log_w = g[..., None] - b + ib
        m_new = jnp.maximum(g + m, jnp.max(log_w, -1))
        w = jnp.exp(log_w - m_new[..., None])
        decay = jnp.exp(g + m - m_new)
        C_new = decay[..., None, None] * C + jnp.einsum('bhs,bhsd,bhse->bhde', w, kb, vb)
        n_new = decay[..., None] * n + jnp.einsum('bhs,bhsd->bhd', w, kb)
        return (C_new, n_new, m_new), h

    init = (jnp.zeros((B, H, dh, dh), jnp.float32), jnp.zeros((B, H, dh), jnp.float32),
            jnp.zeros((B, H), jnp.float32))
    _, hs = lax.scan(step, init, (to_chunks(q), to_chunks(k), to_chunks(v),
                                   to_chunks(i_pre), to_chunks(log_f)))
    return from_chunks(hs)

def retention_chunkwise(q, k, v, log_gamma):
    B, H, T, dh = q.shape
    idx = jnp.arange(CHUNK)
    rel = idx[:, None] - idx[None, :]
    decay_in = jnp.where(rel >= 0, jnp.exp(log_gamma[:, None, None] * jnp.maximum(rel, 0)), 0.0)
    xi = jnp.exp(log_gamma[:, None] * (idx + 1))
    zeta = jnp.exp(log_gamma[:, None] * (CHUNK - 1 - idx))
    g_chunk = jnp.exp(log_gamma * CHUNK)

    def step(R, inp):
        qb, kb, vb = inp
        inner = jnp.einsum('bhld,bhsd->bhls', qb, kb) * decay_in
        y = jnp.einsum('bhls,bhse->bhle', inner, vb) + \
            xi[None, :, :, None] * jnp.einsum('bhld,bhde->bhle', qb, R)
        R_new = g_chunk[None, :, None, None] * R + jnp.einsum('bhsd,hs,bhse->bhde', kb, zeta, vb)
        return R_new, y

    _, ys = lax.scan(step, jnp.zeros((B, H, dh, dh), jnp.float32),
                     (to_chunks(q), to_chunks(k), to_chunks(v)))
    return from_chunks(ys)

def alibi_slopes(n_heads):
    return jnp.exp2(-8.0 * jnp.arange(1, n_heads + 1, dtype=jnp.float32) / n_heads)

def dilated_band_attention(q, k, v, window, dilation, slopes):
    B, T, H, dh = q.shape
    L = window // dilation
    span = L * dilation
    T_pad = -(-T // span) * span
    NB = T_pad // span

    def blocks(a):
        a = jnp.pad(a.astype(jnp.float32), ((0, 0), (0, T_pad - T), (0, 0), (0, 0)))
        return a.reshape(B, NB, L, dilation, H, dh).transpose(0, 3, 4, 1, 2, 5)

    def with_prev(a):
        prev = jnp.pad(a, ((0, 0), (0, 0), (0, 0), (1, 0), (0, 0), (0, 0)))[:, :, :, :-1]
        return jnp.concatenate([prev, a], axis=4)

    qb = blocks(q)
    kk, vv = with_prev(blocks(k)), with_prev(blocks(v))
    qi = jnp.arange(L)[:, None]
    kr = jnp.arange(2 * L)[None, :]
    steps = qi + L - kr
    band = (steps >= 0) & (steps <= L)
    first = (jnp.arange(NB) == 0)[:, None, None]
    valid = band[None] & ~(first & (kr < L)[None])
    bias = -slopes[:, None, None] * (steps * dilation).astype(jnp.float32)
    s = jnp.einsum('brhnqd,brhnkd->brhnqk', qb, kk) * (dh ** -0.5) + bias[:, None]
    s = jnp.where(valid, s, -jnp.inf)
    m = jnp.max(s, -1, keepdims=True)
    p = jnp.exp(s - m)
    den = jnp.sum(p, -1)
    o = jnp.einsum('brhnqk,brhnkd->brhnqd', p, vv) / den[..., None]
    lse = m[..., 0] + jnp.log(den)
    o = o.transpose(0, 3, 4, 1, 2, 5).reshape(B, T_pad, H, dh)[:, :T]
    lse = lse.transpose(0, 3, 4, 1, 2).reshape(B, T_pad, H)[:, :T]
    return o, lse

def even_mixer(x, w_in, i_bias, f_bias, conv_w, conv_b, mlstm_norm_g, ret_norm_g, w_out):
    B, T, _ = x.shape
    f32 = jnp.float32
    p = x @ w_in
    q_m, k_m, v_m, o_m, i_m, f_m, q_r, k_r, v_r, g_r = jnp.split(p, IN0_SPLITS, axis=-1)
    qk_m = jax.nn.silu(causal_depthwise_conv(jnp.concatenate([q_m, k_m], -1), conv_w, conv_b))
    q_m, k_m = jnp.split(qk_m, 2, axis=-1)

    def heads(a, n):
        return a.astype(f32).reshape(B, T, n, HEAD_DIM).transpose(0, 2, 1, 3)

    scale = HEAD_DIM ** -0.5
    i_pre = (i_m + i_bias).astype(f32).transpose(0, 2, 1)
    log_f = jax.nn.log_sigmoid((f_m + f_bias).astype(f32)).transpose(0, 2, 1)
    h_m = mlstm_chunkwise(heads(q_m, MLSTM_HEADS), heads(k_m, MLSTM_HEADS) * scale,
                          heads(v_m, MLSTM_HEADS), i_pre, log_f).transpose(0, 2, 1, 3)
    h_m = jax.nn.sigmoid(o_m.astype(f32)).reshape(B, T, MLSTM_HEADS, HEAD_DIM) * h_m
    y_m = head_norm(h_m, mlstm_norm_g)
    log_gamma = jnp.log1p(-jnp.exp2(-5.0 - jnp.arange(RET_HEADS, dtype=f32)))
    h_r = retention_chunkwise(heads(q_r, RET_HEADS), heads(k_r, RET_HEADS) * scale,
                              heads(v_r, RET_HEADS), log_gamma).transpose(0, 2, 1, 3)
    y_r = head_norm(h_r, ret_norm_g) * jax.nn.silu(g_r.astype(f32))
    y = jnp.concatenate([y_m, y_r], -1).astype(x.dtype)
    return y @ w_out

def odd_mixer(x, w_in, w_out):
    B, T, _ = x.shape
    p = (x @ w_in).reshape(B, T, len(DIL_CONFIGS), 3, DIL_HEADS, DIL_DH)
    slopes = alibi_slopes(DIL_HEADS)
    outs, lses = [], []
    for g, (window, dilation) in enumerate(DIL_CONFIGS):
        o, l = dilated_band_attention(p[:, :, g, 0], p[:, :, g, 1], p[:, :, g, 2],
                                      window, dilation, slopes)
        outs.append(o)
        lses.append(l)
    wts = jax.nn.softmax(jnp.stack(lses, 0), axis=0)
    y = jnp.einsum('gbth,gbthd->bthd', wts, jnp.stack(outs, 0))
    return y.reshape(B, T, DIL_W).astype(x.dtype) @ w_out

def route(h, router_w, router_bias):
    N = h.shape[0]
    aff = jax.nn.sigmoid((h @ router_w).astype(jnp.float32))
    sel = (aff + router_bias.astype(jnp.float32)).reshape(N, N_GROUPS, EXPERTS_PER_GROUP)
    grp_score = jnp.sum(lax.top_k(sel, 2)[0], -1)
    g_best = jnp.argmax(grp_score, -1)
    in_grp = jnp.take_along_axis(sel, g_best[:, None, None], axis=1)[:, 0]
    _, local = lax.top_k(in_grp, TOP_K)
    expert_idx = g_best[:, None] * EXPERTS_PER_GROUP + local
    gate = jnp.take_along_axis(aff, expert_idx, axis=1)
    return expert_idx, gate / jnp.sum(gate, -1, keepdims=True)

def moe_ffn(h, router_w, router_bias, w_gate, w_up, w_down):
    B, T, D = h.shape
    N = B * T
    hf = h.reshape(N, D)
    expert_idx, gate = route(hf, router_w, router_bias)
    M = N * TOP_K
    e_flat = expert_idx.reshape(M)
    tok_flat = jnp.repeat(jnp.arange(N, dtype=jnp.int32), TOP_K)
    g_flat = gate.reshape(M)
    order = jnp.argsort(e_flat)
    e_s, tok_s, g_s = e_flat[order], tok_flat[order], g_flat[order]
    counts = jnp.bincount(e_flat, length=N_EXPERTS)
    padded = (counts + MOE_BLOCK - 1) // MOE_BLOCK * MOE_BLOCK
    start = jnp.cumsum(counts) - counts
    pend = jnp.cumsum(padded)
    pstart = pend - padded
    dest = pstart[e_s] + (jnp.arange(M) - start[e_s])
    P = M + N_EXPERTS * MOE_BLOCK
    slot_tok = jnp.zeros((P,), jnp.int32).at[dest].set(tok_s)
    slot_gate = jnp.zeros((P,), jnp.float32).at[dest].set(g_s)
    n_blocks = P // MOE_BLOCK
    block_e = jnp.minimum(jnp.searchsorted(pend, jnp.arange(n_blocks) * MOE_BLOCK, side='right'),
                          N_EXPERTS - 1)
    xs = hf[slot_tok].reshape(n_blocks, MOE_BLOCK, D)

    def expert_block(args):
        xb, e = args
        return (jax.nn.silu(xb @ w_gate[e]) * (xb @ w_up[e])) @ w_down[e]

    ys = lax.map(expert_block, (xs, block_e)).reshape(P, D)
    out = jnp.zeros((N, D), ys.dtype).at[slot_tok].add(ys * slot_gate[:, None].astype(ys.dtype))
    return out.reshape(B, T, D)

def setup_inputs(seed: int = 0) -> dict:
    key = jax.random.key(seed)
    ks = jax.random.split(key, 18)
    f32 = jnp.float32

    def nrm(k, shape, scale):
        return jax.random.normal(k, shape, f32) * scale

    return {
        "x": nrm(ks[0], (BATCH, SEQ, D_MODEL), 1.0),
        "w_in_even": nrm(ks[1], (N_EVEN, D_MODEL, IN0_COLS), D_MODEL ** -0.5),
        "i_bias": nrm(ks[2], (N_EVEN, MLSTM_HEADS), 0.1),
        "f_bias": jnp.linspace(3.0, 6.0, MLSTM_HEADS)[None] + nrm(ks[3], (N_EVEN, MLSTM_HEADS), 0.1),
        "conv_w": nrm(ks[4], (N_EVEN, CONV_WIDTH, 2 * MLSTM_W), CONV_WIDTH ** -0.5),
        "conv_b": nrm(ks[5], (N_EVEN, 2 * MLSTM_W), 0.02),
        "mlstm_norm_g": 1.0 + nrm(ks[6], (N_EVEN, MLSTM_W), 0.02),
        "ret_norm_g": 1.0 + nrm(ks[7], (N_EVEN, RET_W), 0.02),
        "w_out_even": nrm(ks[8], (N_EVEN, MLSTM_W + RET_W, D_MODEL), (MLSTM_W + RET_W) ** -0.5 * BETA),
        "w_in_odd": nrm(ks[9], (N_ODD, D_MODEL, IN1_COLS), D_MODEL ** -0.5),
        "w_out_odd": nrm(ks[10], (N_ODD, DIL_W, D_MODEL), DIL_W ** -0.5 * BETA),
        "router_w": nrm(ks[11], (D_MODEL, N_EXPERTS), D_MODEL ** -0.5),
        "router_bias": nrm(ks[12], (N_EXPERTS,), 0.01),
        "w_gate": nrm(ks[13], (DEPTH, N_EXPERTS, D_MODEL, D_EXPERT), D_MODEL ** -0.5),
        "w_up": nrm(ks[14], (DEPTH, N_EXPERTS, D_MODEL, D_EXPERT), D_MODEL ** -0.5),
        "w_down": nrm(ks[15], (DEPTH, N_EXPERTS, D_EXPERT, D_MODEL), D_EXPERT ** -0.5 * BETA),
        "ln_g": 1.0 + nrm(ks[16], (DEPTH, 2, D_MODEL), 0.02),
        "ln_b": nrm(ks[17], (DEPTH, 2, D_MODEL), 0.02),
    }

def reference(x, w_in_even, i_bias, f_bias, conv_w, conv_b, mlstm_norm_g, ret_norm_g,
              w_out_even, w_in_odd, w_out_odd, router_w, router_bias, w_gate, w_up,
              w_down, ln_g, ln_b):
    h = x
    for layer in range(DEPTH):
        j = layer // 2
        if layer % 2 == 0:
            mix = even_mixer(h, w_in_even[j], i_bias[j], f_bias[j], conv_w[j], conv_b[j],
                             mlstm_norm_g[j], ret_norm_g[j], w_out_even[j])
        else:
            mix = odd_mixer(h, w_in_odd[j], w_out_odd[j])
        h = layer_norm(ALPHA * h + mix, ln_g[layer, 0], ln_b[layer, 0])
        ffn = moe_ffn(h, router_w, router_bias, w_gate[layer], w_up[layer], w_down[layer])
        h = layer_norm(ALPHA * h + ffn, ln_g[layer, 1], ln_b[layer, 1])
    return h


_drawn_inputs = setup_inputs


def setup_inputs(seed=0):
    import zlib

    import numpy as np

    out = dict(_drawn_inputs(seed))
    spreads = {}
    factors = {'i_bias': 200.0, 'conv_b': 3.12, 'ret_norm_g': 3.468}
    for name, (base, spread) in spreads.items():
        noise = np.random.default_rng([zlib.crc32(name.encode()), seed]).standard_normal(out[name].shape)
        drawn = base * np.exp(spread * noise) if base else spread * noise
        out[name] = __import__('jax').numpy.asarray(drawn.astype(out[name].dtype))
    for name, factor in factors.items():
        out[name] = (out[name] * factor).astype(out[name].dtype)
    return out
```

```python
import concourse.bass as bass
from concourse import mybir
from contextlib import ExitStack, contextmanager


class Count:

    def __init__(self, eng, name="count"):
        self.eng, self.reg = eng, eng.alloc_register(name)

    def wait(self, sem, value, met):
        self.eng.reg_mov(self.reg, value)
        value = self.eng.snap(self.reg)
        self.eng.wait_ge(met, 1)
        self.eng.wait_ge(sem, value)


class Order:

    def __init__(self, eng, sem, count=None):
        self.eng, self.sem, self.n, self.loop = eng, sem, 0, None
        self.count = count or Count(eng)

    def __call__(self, ins, plain=False):
        self.n += 1
        ins.then_inc(self.sem, 1)
        value = self.n if self.loop is None else self.loop + self.n
        if plain:
            self.count.wait(self.sem, value, self.sem)
        else:
            self.eng.wait_ge(self.sem, value)

    @contextmanager
    def rolled(self, i, per_iter, iters):
        start = self.n
        self.loop, self.n = i * per_iter + start, 0
        yield
        assert self.n == per_iter, f"{self.n} links per iteration, not {per_iter}"
        self.loop, self.n = None, start + per_iter * iters


def trunk(nc, x, w_in_even, i_bias, f_bias, conv_w, conv_b, mlstm_norm_g, ret_norm_g, w_out_even,
          w_in_odd, w_out_odd, router_w, router_bias, w_gate, w_up, w_down, ln_g, ln_b, out):
    f32, f32r, bf16 = mybir.dt.float32, mybir.dt.float32r, mybir.dt.bfloat16
    i32, u32 = mybir.dt.int32, mybir.dt.uint32
    ALU, ACT, AX = mybir.AluOpType, mybir.ActivationFunctionType, mybir.AxisListType
    ds = bass.ds

    P = 128
    T, D = x.shape[1], x.shape[2]
    NT, KT = T // P, D // P
    HD = D // 8
    NH = 4
    VW = HD + 1
    DH = D // 16
    E, EG = w_gate.shape[1], 8
    F = w_gate.shape[3]
    B = 64
    NBLK = 48
    NPAIR = NBLK // 2
    NCOL = NPAIR + 2
    EMPTY = 4096
    ALPHA = 4.0 ** 0.25
    EPS = 1e-5
    BIG = 1e30
    C = 512
    SCALE = HD ** -0.5
    OFF = (0, 512, 896, 1152)
    IN_QR = 4 * NH * HD + 2 * NH
    GATE0 = 4 * NH * HD
    LOG_GAMMA = [-0.03174869831458027, -0.01574835696813892, -0.007843177461025893, -0.003913899321136329]
    SLOPES = [2.0 ** -(h + 1) for h in range(8)]

    ctx = ExitStack()
    with ctx:
        KB = 1024
        BASE = 20 * KB

        class Zone:
            def __init__(self, start, size):
                self.at, self.end = start, start + size

            def take(self, name, shape, dt):
                n = 1
                for s in shape[1:]:
                    n *= s
                n *= 2 if dt == bf16 else 4
                t = nc.alloc_sbuf_tensor_at(name, shape, dt, offset=self.at)
                self.at += (n + 31) // 32 * 32
                assert self.at <= self.end, name
                return t

        const = Zone(BASE, 18 * KB)
        ident = const.take("ident", [P, P], f32)
        dist = const.take("dist", [P, T], f32)
        mask = const.take("mask", [P, P], f32)
        near = const.take("near", [P, 2, 256], f32)
        before = const.take("before", [P, P], bf16)
        ones_bf = const.take("ones_bf", [P, P], bf16)
        rw = const.take("rw", [P, KT, E], f32)
        rb = const.take("rb", [P, E], f32)
        row128 = const.take("row128", [P, P], f32)
        thr = const.take("thr", [P, 8], f32)
        tok_of = const.take("tok_of", [P, 2, NT], f32)
        dst_of = const.take("dst_of", [P, 2, NT], f32)
        lgam = const.take("lgam", [P, NH], f32)
        nslope = const.take("nslope", [P, 8], f32)
        cw = const.take("cw", [P, 8, 5], f32)
        gb = const.take("gb", [64, 1], f32)
        sel4 = const.take("sel4", [4, NH, P], f32)
        cwr = Zone(const.at, 4 * KB).take("cwr", [5, D], f32)
        lngb = const.take("lngb", [P, 2, D], f32)
        stat = const.take("stat", [P, 8, 6], f32)
        mv = const.take("mv", [P, 8, 2], f32)
        rstd = const.take("rstd", [P, 8], f32)
        nmr = const.take("nmr", [P, 8], f32)
        nwt = const.take("nwt", [P, 8], f32)
        one = const.take("one", [P, 1], f32)
        h = Zone(BASE + 18 * KB, 16 * KB).take("h", [P, NT, D], f32)

        XZ = BASE + 34 * KB
        z = Zone(XZ, 32 * KB)
        xt_hi = z.take("xt_hi", [P, KT, T], f32r)
        xt_lo = z.take("xt_lo", [P, KT, T], f32r)
        z = Zone(XZ, 32 * KB)
        ks = [z.take(f"ks{i}", [P, T], f32) for i in range(2)]
        pt = [z.take(f"pt{i}", [P, 1280], f32) for i in range(2)]
        dd = [z.take(f"dd{i}", [P, 1280], f32) for i in range(2)]
        mbd = [z.take(f"mbd{i}", [P, NT, P], f32) for i in range(2)]
        hm = [z.take(f"hm{i}", [P, NT, HD], f32) for i in range(2)]
        z = Zone(XZ, 32 * KB)
        qz = [z.take(f"qz{i}", [P, 3, T], f32) for i in range(2)]
        sc = [z.take(f"sc{i}", [P, NT, 256], f32) for i in range(2)]
        ptt = [z.take(f"ptt{i}", [P, NT, 256], f32) for i in range(2)]
        bh = [z.take(f"bh{i}", [P, 2, 256], f32) for i in range(2)]
        z = Zone(XZ, 32 * KB)
        ht = z.take("ht", [P, KT, T], f32)
        aoh = z.take("aoh", [P, 8, P], f32)
        bv = z.take("bv", [P, 8, 3 * NCOL], f32)
        cmp = z.take("cmp", [1, NBLK, E], f32)

        R = BASE + 66 * KB
        z = Zone(R, 48 * KB)
        raw = [z.take(f"raw{i}", [P, 4, C], f32) for i in range(2)]
        wh = [z.take(f"wh{i}", [P, 4, C], f32r) for i in range(2)]
        wl = [z.take(f"wl{i}", [P, 4, C], f32r) for i in range(2)]
        z = Zone(R + 48 * KB, 90 * KB)
        qk = z.take("qk", [P, 2, 2, NH, T], f32)
        v = z.take("v", [P, 2, NT, NH, VW], f32)
        og = z.take("og", [P, 2, NT, NH * HD], f32)
        mb = z.take("mb", [P, NH, T], f32)
        rows = z.take("rows", [64, T], f32)
        mrow = z.take("mrow", [4, T], f32)
        zf = z.take("zf", [4, T], f32)
        ex = z.take("ex", [4, T], f32)
        gn = z.take("gn", [P, 2, NH * HD], f32)
        cta = z.take("cta", [P, T], f32)
        ctb = z.take("ctb", [P, T], f32)
        jdiff = z.take("jdiff", [P, P], i32)
        z = Zone(R + 48 * KB, 90 * KB)
        q3 = z.take("q3", [P, 3, 4, T], f32)
        k3 = z.take("k3", [P, 3, 4, T], f32)
        v3 = z.take("v3", [P, 3, NT, 8 * DH], f32)
        ms = z.take("ms", [P, 2, NT, 8], f32)
        dn = z.take("dn", [P, 2, NT, 8], f32)
        me = z.take("me", [P, NT, 16], f32)
        mx = z.take("mx", [P, NT, 8], f32)
        w1 = z.take("w1", [P, NT, 8], f32)
        w2 = z.take("w2", [P, NT, 8], f32)
        dsum = z.take("dsum", [P, NT, 8], f32)
        mm = [z.take(f"mm{i}", [P, NT], f32) for i in range(2)]
        nm = [z.take(f"nm{i}", [P, NT], f32) for i in range(2)]
        z = Zone(R, 138 * KB)
        wgu = z.take("wgu", [P, 2, 2, 2, KT, F], f32)
        wd = z.take("wd", [P, 2, 2, 2, D], f32)
        y2z = Zone(z.at, 16 * KB)
        xg = [z.take(f"xg{i}", [P, D], f32) for i in range(2)]
        xgt = [z.take(f"xgt{i}", [P, KT, P], f32) for i in range(2)]
        y2 = [y2z.take(f"y2{i}", [P, 2 * D], f32) for i in range(2)]
        sg = [z.take(f"sg{i}", [P, F], f32) for i in range(2)]
        hh = [z.take(f"hh{i}", [P, F], f32) for i in range(2)]
        htt = [z.take(f"htt{i}", [P, 2, P], f32) for i in range(2)]
        yt = [z.take(f"yt{i}", [P, D], f32) for i in range(2)]
        aff = z.take("aff", [P, NT, E], f32)
        sel = z.take("sel", [P, NT, E], f32)
        msel = z.take("msel", [P, NT, E], f32)
        m8g = z.take("m8g", [P, NT, 4, 8], f32)
        gs = z.take("gs", [P, NT, 8], f32)
        gm = z.take("gm", [P, NT, 8], f32)
        gi = z.take("gi", [P, NT, 8], u32)
        gif = z.take("gif", [P, NT], f32)
        pen = z.take("pen", [P, NT, 4], f32)
        v8 = z.take("v8", [P, NT, 8], f32)
        i8 = z.take("i8", [P, NT, 8], u32)
        ef = z.take("ef", [P, 2, NT], f32)
        oh = z.take("oh", [P, 2, NT, E], f32)
        ohs = z.take("ohs", [P, NT, E], bf16)
        t1 = z.take("t1", [P, 2, NT, E], f32)
        ga = z.take("ga", [P, 2, NT], f32)
        gd = z.take("gd", [P, NT], f32)
        cm = z.take("cm", [P, E, 8], f32)
        nb = z.take("nb", [P, E], f32)
        bend = z.take("bend", [P, E], f32)
        bst = z.take("bst", [P, E], f32)
        ber = z.take("ber", [1, NBLK], f32)
        be = z.take("be", [1, NBLK], i32)
        ni = z.take("ni", [1, 3], i32)
        pos = z.take("pos", [P, NT, E], f32)
        dest = z.take("dest", [P, 8], f32)
        di = z.take("di", [P, 8], i32)
        pf = z.take("pf", [P, 8], f32)
        rm = z.take("rm", [P, 8], f32)
        eq = z.take("eq", [P, 8, NCOL], f32)
        ti = z.take("ti", [P, NCOL], i32)
        td = z.take("td", [P, NCOL], i32)
        gt = z.take("gt", [P, NCOL], f32)
        gidx = [z.take(f"gidx{i}", [P, 1], i32) for i in range(2)]
        sidx = [z.take(f"sidx{i}", [P, 1], i32) for i in range(2)]
        z = Zone(20480 - 3 * KB, 3 * KB)
        g64 = z.take("g64", [P, NT, 64], f32)
        uc = z.take("uc", [P, NT, 64], f32)
        en = z.take("en", [P, NT, NH], f32)
        wif = z.take("wif", [P, KT, 8], f32)
        wif_hi = z.take("wif_hi", [P, KT, 8], f32r)
        wif_lo = z.take("wif_lo", [P, KT, 8], f32r)

        bank = [ctx.enter_context(nc.psum_tensor(f"bank{i}", [P, 512], f32)) for i in range(8)]

        h_rows = [nc.dram_tensor(f"h_rows{i}", [T, D], f32).ap() for i in range(2)]
        y_rows = [nc.dram_tensor(f"y_rows{i}", [2 * T, D], f32).ap() for i in range(2)]
        SR = 8 * DH + 16
        far = nc.dram_tensor("far_rows", [T, SR], f32).ap()

        def sem(name):
            return ctx.enter_context(nc.semaphore(name))

        x_in, gate_in, cw_in, gb_in, gn_in, rw_in = (sem(s) for s in
            ("x_in", "gate_in", "cw_in", "gb_in", "gn_in", "rw_in"))
        ln_in = sem("ln_in")
        consts = sem("consts_ready")
        xt_ps, xt_h, xt_l = sem("xt_in_psum"), sem("xt_hi_ready"), sem("xt_lo_ready")
        raw_in = [sem("raw_in0"), sem("raw_in1")]
        w_hi, w_lo = sem("w_hi_ready"), sem("w_lo_ready")
        unit_done = sem("unit_done")
        ev_a, ev_d = sem("evacuated_act"), sem("evacuated_dve")
        act_o, dve_o, pool_o = sem("act_order"), sem("dve_order"), sem("pool_order")
        gate_hi, gate_lo, gate_ps, gate_sb, gate_tr = (sem(s) for s in
            ("gate_w_hi", "gate_w_lo", "gate_in_psum", "gate_in_sbuf", "gate_rows_in_psum"))
        gate_exp, gate_ln, rows_ready = sem("gate_neg_abs"), sem("gate_softplus"), sem("rows_ready")
        cw_ps, cw_sb = sem("conv_taps_in_psum"), sem("conv_taps_ready")
        conv_done, silu_done = sem("conv_done"), sem("qk_silu_done")
        og_act, og_ready = sem("output_gates_act"), sem("output_gates_ready")
        mb_ps, mb_sb, uc_ps, uc_sb, en_sb = (sem(s) for s in
            ("m_rows_in_psum", "m_rows_ready", "u_cols_in_psum", "u_cols_ready", "exp_neg_m_ready"))
        ks_ready, s_ready, d_ready, pt_ready, o_ready = (sem(s) for s in
            ("k_staged", "scores_ready", "decay_ready", "weights_ready", "heads_out_ready"))
        mbd_ready, o_read, yn_ready, y_done = (sem(s) for s in
            ("masked_m_ready", "heads_out_read", "head_normed", "y_done"))
        ln_in_ready, ln_nmr, ln_norm, ln_scaled, ln_out = (sem(s) for s in
            ("residual_ready", "ln_coeffs", "ln_normed", "ln_scaled", "ln_out"))
        h_stored = sem("h_stored")
        rt_ps, rt_sb, lg_ps, aff_ready = (sem(s) for s in
            ("router_xt_in_psum", "router_xt_ready", "logits_in_psum", "affinities_ready"))
        oh_ready, cnt_ps, blk_ready, ab_ready, tb_ps, tb_ready = (sem(s) for s in
            ("onehots_ready", "counts_in_psum", "blocks_ready", "table_terms_ready",
             "tables_in_psum", "tables_ready"))
        wgu_in = [[sem(f"gate_up_in{l}{i}") for i in range(2)] for l in range(2)]
        wd_in = [[sem(f"down_in{l}{i}") for i in range(2)] for l in range(2)]
        xg_in = [[sem(f"rows_gathered{l}{i}") for i in range(2)] for l in range(2)]
        y_out = [[sem(f"rows_scattered{l}{i}") for i in range(2)] for l in range(2)]
        (xg_tr, xgt_a, xgt_d, gu_done, sg_ready, hh_ready, ht_tr, ht_sb, dn_done, ya_ready,
         yd_ready, idx_ready, moe_done) = (
            [sem(f"{s}{l}") for l in range(2)] for s in
            ("xg_transposed", "xgt_ready_act", "xgt_ready_dve", "gate_up_done", "silu_ready",
             "hidden_ready", "hidden_transposed", "hidden_t_ready", "down_done", "y_ready_act",
             "y_ready_dve", "pool_indices", "moe_done"))
        y2_in = [sem("y2_in0"), sem("y2_in1")]
        y2_read = sem("y2_read")
        bh_ready, qz_ready = sem("bias_ready"), sem("q_staged")
        s2_ready, sb_ready, nm_ready, p_ready = (sem(s) for s in
            ("odd_scores", "odd_biased", "odd_neg_max", "odd_weights"))
        t_ready, pta, ptd, o2_ready, oe_ready = (sem(s) for s in
            ("odd_weights_t", "odd_wt_act", "odd_wt_dve", "odd_out", "odd_out_kept"))
        far_out, far_in = sem("far_rows_stored"), sem("far_rows_loaded")
        mx_ready, we_ready, wn_ready, far_scaled, yo_ready = (sem(s) for s in
            ("merge_max", "merge_exp", "merge_weights", "far_scaled", "odd_y_ready"))
        out_stored = sem("out_stored")
        first_right, reloaded = sem("first_weights_right"), [sem(f"first_weights_reloaded{l}") for l in range(2)]

        xe, xo = w_in_even[0], w_in_odd[0]
        woe, woo = w_out_even[0], w_out_odd[0]
        U_WOUT, U_ODD, U_ODDV, U_WOUT2 = 16, 20, 32, 38

        def unit_src(w, row0, col):
            return w[row0:row0 + 4 * P, col].rearrange("(k p) c -> p k c", p=P)

        def perm(ap):
            return ap.rearrange("p (j a) -> p a j", a=4)

        block = ctx.enter_context(nc.Block())

        @block.sync
        def _(sp):
            sp.dma_start(h[:, :, :], x[0].rearrange("(t p) d -> p t d", p=P)).then_inc(x_in, 16)

            def load_unit(u, slot, w, row0, col):
                sp.wait_ge(w_lo, u + 1)
                sp.dma_start(raw[slot][:, :, :], unit_src(w, row0, col)).then_inc(raw_in[slot], 16)

            def load_ln(n):
                if n:
                    sp.wait_ge(ln_out, 4 * n)
                for i, w in enumerate((ln_g, ln_b)):
                    sp.dma_start(lngb[:, i, :], w[n // 2, n % 2:n % 2 + 1, :].to_broadcast([P, D]))\
                      .then_inc(ln_in, 16)

            def store_h(n):
                for t in range(NT):
                    sp.wait_ge(ln_out, 4 * n + t + 1)
                    sp.dma_start(h_rows[n // 2][t * P:(t + 1) * P, :], h[:, t, :]).then_inc(h_stored, 16)

            def load_gate_up(l, par, experts, done):
                for b, e in enumerate(experts):
                    for i, w in enumerate((w_gate, w_up)):
                        sp.dma_start(wgu[:, par, b, i, :, :].rearrange("p k f -> p (k f)"),
                                     w[l][ds(e, 1)].rearrange("a (p k) f -> p (a k f)", p=P)).then_inc(done, 16)

            def load_down(l, par, experts, done):
                for b, e in enumerate(experts):
                    sp.dma_start(wd[:, par, b, :, :].rearrange("p k n -> p (k n)"),
                                 w_down[l][ds(e, 1)].rearrange("a (p k) n -> p (a k n)", p=P)).then_inc(done, 16)

            def early_down(l):
                for par in range(2):
                    load_down(l, par, (2 * par, 2 * par + 1), wd_in[l][par])

            def early_gate_up(l):
                for par in range(2):
                    load_gate_up(l, par, (2 * par, 2 * par + 1), wgu_in[l][par])

            def expert_weights(l):
                sp.wait_ge(blk_ready, l + 1)
                iters = sp.value_load(ni[0:1, 1:2], min_val=1, max_val=NBLK // 4)
                wrong = sp.value_load(ni[0:1, 2:3], min_val=0, max_val=1)

                def block_experts(j):
                    return [sp.value_load(be[0:1, ds(j + b, 1)], min_val=0, max_val=E - 1) for b in range(2)]

                with sp.If(wrong > 0):
                    for par in range(2):
                        sp.wait_ge(wgu_in[l][par], 64)
                        sp.wait_ge(wd_in[l][par], 32)
                    for par in range(2):
                        e = block_experts(2 * par)
                        load_gate_up(l, par, e, reloaded[l])
                        load_down(l, par, e, reloaded[l])
                    sp.wait_ge(reloaded[l], 12 * 16)
                sp.sem_inc(first_right, 1)
                with sp.Fori(1, iters) as it:
                    for par in range(2):
                        e = block_experts(4 * it + 2 * par)
                        sp.wait_ge(gu_done[l], 2 * it + par + 1)
                        load_gate_up(l, par, e, wgu_in[l][par])
                        sp.wait_ge(dn_done[l], 2 * it + par + 1)
                        load_down(l, par, e, wd_in[l][par])

            def load_y(l):
                sp.wait_ge(moe_done[l], 1)
                for t in range(NT):
                    if t >= 2:
                        sp.wait_ge(y2_read, NT * l + t - 1)
                    sp.dma_start(y2[t % 2][:, :], y_rows[l][2 * t * P:2 * (t + 1) * P, :]
                                 .rearrange("(p c) d -> p (c d)", c=2)).then_inc(y2_in[t % 2], 16)

            with sp.Fori(0, 2) as j:
                for i in range(4):
                    for half in range(2):
                        load_unit(8 * j + 2 * i + half, half, xe, half * 4 * P, ds(j * IN_QR + i * C, C))
            load_ln(0)
            for c in range(2):
                for half in range(2):
                    load_unit(U_WOUT + 2 * c + half, half, woe, half * 4 * P, slice(c * C, (c + 1) * C))
            sp.wait_ge(o_ready, 8 + 2)
            early_down(0)
            sp.wait_ge(unit_done, U_ODD + 2)
            early_gate_up(0)
            store_h(0)
            load_ln(1)
            expert_weights(0)
            load_y(0)
            with sp.Fori(0, 3) as g:
                for i in range(2):
                    for half in range(2):
                        load_unit(4 * g + (U_ODD + 2 * i + half), half, xo, half * 4 * P,
                                  ds(g * (3 * C) + i * C, C))
            for g in range(3):
                for half in range(2):
                    load_unit(U_ODDV + 2 * g + half, half, xo, half * 4 * P,
                              slice(3 * C * g + 2 * C, 3 * C * (g + 1)))
            for c in range(2):
                load_unit(U_WOUT2 + c, c, woo, 0, slice(c * C, (c + 1) * C))
            load_ln(2)
            farv = far.rearrange("(j a) c -> j a c", a=4)
            for hp in range(4):
                sp.wait_ge(oe_ready, 4 * hp + 4 + 2)
                sp.dma_start(farv[:, :, 2 * DH * hp:2 * DH * (hp + 1)],
                             q3[:, 1, hp, :].rearrange("p (a c) -> p a c", a=NT)).then_inc(far_out, 16)
            sp.dma_start(farv[:, :, 8 * DH:8 * DH + 8], ms[:, 1, :, :]).then_inc(far_out, 16)
            sp.dma_start(farv[:, :, 8 * DH + 8:], dn[:, 1, :, :]).then_inc(far_out, 16)
            sp.wait_ge(far_out, 6 * 16)
            fart = far.rearrange("(t p) c -> p t c", p=P)
            sp.dma_start(me[:, :, :], fart[:, :, 8 * DH:]).then_inc(far_in, 16)
            sp.dma_start(q3[:, 2, :, :], fart[:, :, 0:8 * DH]).then_inc(far_in, 16)
            sp.wait_ge(yo_ready, 4)
            early_down(1)
            sp.wait_ge(unit_done, U_WOUT2 + 2 + 2)
            early_gate_up(1)
            store_h(2)
            load_ln(3)
            expert_weights(1)
            load_y(1)
            for t in range(NT):
                sp.wait_ge(ln_out, 12 + t + 1)
                sp.dma_start(out[0, t * P:(t + 1) * P, :], h[:, t, :]).then_inc(out_stored, 16)
            sp.wait_ge(out_stored, 16 * NT)
            sp.wait_ge(h_stored, 16 * 2 * NT)

        @block.gpsimd
        def _(pool):
            link = Order(pool, pool_o)
            column_reg = pool.alloc_register("column")

            def column(value):
                pool.reg_mov(column_reg, value)
                return pool.snap(column_reg, min_val=0, max_val=NCOL - 1)

            pool.sem_inc(y_done, 2)
            for t in (ident, mask):
                pool.memset(t[:, :], 0.0)
            pool.memset(before[:, :], 1.0)
            pool.memset(ones_bf[:, :], 1.0)
            pool.memset(one[:, :], 1.0)
            pool.memset(g64[:, :, :], 0.0)
            pool.memset(rows[:, :], 0.0)
            pool.memset(sel4[:, :, :], 0.0)
            pool.memset(near[:, :, :], BIG)
            pool.memset(v[:, 0, :, :, HD:VW], 1.0)
            pool.memset(v[:, 1, :, :, HD:VW], 1.0)
            for i in range(NH):
                pool.memset(lgam[:, i:i + 1], LOG_GAMMA[i])
            for i in range(8):
                pool.memset(nslope[:, i:i + 1], -SLOPES[i])
                pool.memset(thr[:, i:i + 1], float(B * i))
            exact = dict(allow_small_or_imprecise_dtypes=True)
            pool.iota(dist[:, :], pattern=[[1, T]], base=0, channel_multiplier=-1, **exact)
            pool.iota(row128[:, :], pattern=[[1, P]], base=0, channel_multiplier=0, **exact)
            pool.iota(tok_of[:, :, :], pattern=[[0, 2], [P, NT]], base=-EMPTY, channel_multiplier=1, **exact)
            link(pool.iota(dst_of[:, :, :], pattern=[[1, 2], [2 * P, NT]], base=-EMPTY,
                           channel_multiplier=2, **exact))
            pool.affine_select(out=ident[:, :], in_=ident[:, :], compare_op=ALU.not_equal, fill=1.0,
                               base=0, pattern=[[-1, P]], channel_multiplier=1)
            pool.affine_select(out=mask[:, :], in_=mask[:, :], compare_op=ALU.is_ge, fill=BIG,
                               base=0, pattern=[[1, P]], channel_multiplier=-1)
            pool.affine_select(out=before[:, :], in_=before[:, :], compare_op=ALU.is_gt, fill=0.0,
                               base=0, pattern=[[1, P]], channel_multiplier=-1)
            pool.affine_select(out=sel4[:, :, :], in_=sel4[:, :, :], compare_op=ALU.not_equal, fill=1.0,
                               base=0, pattern=[[-1, NH], [0, P]], channel_multiplier=1)
            pool.affine_select(out=dist[:, :], in_=dist[:, :], compare_op=ALU.is_ge, fill=BIG,
                               base=0, pattern=[[1, T]], channel_multiplier=-1)
            link(pool.iota(near[:, 0, :], pattern=[[-1, 256]], base=P, channel_multiplier=1, **exact))
            link(pool.affine_select(out=near[:, 0, :], in_=near[:, 0, :], compare_op=ALU.is_ge, fill=BIG,
                                    base=P, pattern=[[-1, 256]], channel_multiplier=1))
            link(pool.affine_select(out=near[:, 0, :], in_=near[:, 0, :], compare_op=ALU.is_ge, fill=BIG,
                                    base=0, pattern=[[1, 256]], channel_multiplier=-1))
            for c in (0, P):
                pool.iota(near[:, 1, c:c + P], pattern=[[-4, P]], base=0, channel_multiplier=4, **exact)
            link(pool.iota(jdiff[:, :], pattern=[[-1, P]], base=P, channel_multiplier=1))
            for c in (0, P):
                last = pool.affine_select(out=near[:, 1, c:c + P], in_=near[:, 1, c:c + P],
                                          compare_op=ALU.is_ge, fill=BIG, base=0, pattern=[[-4, P]],
                                          channel_multiplier=4)
            last.then_inc(consts, 1)

            pool.wait_ge(cw_sb, 1)
            pool.wait_ge(ev_a, 2 + 2)
            pool.wait_ge(ev_d, 2 + 2)
            qk_m = qk[:, 0, :, :, :].rearrange("p a h t -> p (a h) t")
            pool.wait_ge(consts, 1)
            with pool.Fori(0, 8) as i, link.rolled(i, 9, 8):
                xi = qk_m[:, ds(i, 1), :].rearrange("p a t -> p (a t)")

                def tap(m, n):
                    return cw[:, ds(i, 1), m:m + 1].rearrange("p a b -> p (a b)").to_broadcast([P, n])

                link(pool.tensor_tensor(cta[:, :], xi, tap(3, T), ALU.mult))
                link(pool.tensor_tensor(cta[:, :], cta[:, :], tap(4, T), ALU.add))
                for s in (1, 2, 3):
                    link(pool.tensor_tensor(ctb[:, s:T], xi[:, 0:T - s], tap(3 - s, T - s), ALU.mult))
                    link(pool.tensor_tensor(cta[:, s:T], cta[:, s:T], ctb[:, s:T], ALU.add), plain=(s == 3))
                link(pool.tensor_copy(xi, cta[:, :]))
            pool.tensor_copy(ctb[:, 0:1], cta[:, 0:1]).then_inc(conv_done, 1)

            pool.wait_ge(og_act, 1)
            pool.wait_ge(gn_in, 32)
            pool.tensor_tensor(og[:, 1, :, :], og[:, 1, :, :],
                               gn[:, 1:2, :].to_broadcast([P, NT, NH * HD]), ALU.mult).then_inc(og_ready, 1)
            pool.wait_ge(og_ready, 1)

            def head_gain(branch, base):
                with pool.Fori(0, 2) as i:
                    if branch == 0:
                        for par in range(2):
                            hd = 2 * i + par
                            pool.wait_ge(d_ready, 2 * i + (base + par + 1))
                            pool.tensor_tensor(
                                mbd[par][:, :, :],
                                mb[:, ds(hd, 1), :].rearrange("p a (j t) -> p (a j) t", t=P),
                                mask[:, None, :].to_broadcast([P, NT, P]), ALU.add).then_inc(mbd_ready, 1)
                    for par in range(2):
                        hd = 2 * i + par
                        pool.wait_ge(yn_ready, 2 * i + (base + par + 1))
                        dst = og[:, branch, :, ds(hd * HD, HD)]
                        other = dst if branch else gn[:, 0:1, ds(hd * HD, HD)].to_broadcast([P, NT, HD])
                        pool.tensor_tensor(dst, hm[par][:, :, :], other, ALU.mult).then_inc(y_done, 1)

            head_gain(1, 0)
            pool.wait_ge(mb_sb, 1)
            head_gain(0, NH)

            def ln_shift(n):
                pool.wait_ge(ln_in, 32 * (n + 1))
                for t in range(NT):
                    pool.wait_ge(ln_scaled, 4 * n + t + 1)
                    pool.tensor_tensor(h[:, t, :], h[:, t, :], lngb[:, 1, :], ALU.add).then_inc(ln_out, 1)

            def dispatch(l):
                pool.wait_ge(tb_ready, l + 1)
                pool.wait_ge(h_stored, 16 * NT * (l + 1))
                moved = Order(pool, idx_ready[l], link.count)
                iters = pool.value_load(ni[0:1, 1:2], min_val=1, max_val=NBLK // 4)

                def gather(par):
                    pool.indirect_dma_start(
                        out=xg[par][:, :], out_offset=None, in_=h_rows[l],
                        in_offset=bass.IndirectOffsetOnAxis(ap=gidx[par][:, 0:1], axis=0),
                        bounds_check=T - 1, oob_is_err=False).then_inc(xg_in[l][par], 16)

                def scatter(par, rows_of):
                    pool.indirect_dma_start(
                        out=y_rows[l], out_offset=bass.IndirectOffsetOnAxis(ap=sidx[par][:, 0:1], axis=0),
                        in_=rows_of[:, :], in_offset=None,
                        bounds_check=2 * T - 1, oob_is_err=False).then_inc(y_out[l][par], 16)

                for par in range(2):
                    moved(pool.memset(xg[par][:, :], 0.0))
                    moved(pool.tensor_copy(sidx[par][:, :], td[:, NCOL - 1:NCOL]))
                    scatter(par, xg[par])
                for par in range(2):
                    pool.wait_ge(y_out[l][par], 16)
                    moved(pool.tensor_copy(gidx[par][:, :], ti[:, par:par + 1]))
                    gather(par)
                with pool.Fori(0, iters) as it, moved.rolled(it, 4, 0):
                    for par in range(2):
                        col = column(2 * it + (par + 2))
                        link.count.wait(xg_tr[l], 2 * it + (par + 1), consts)
                        moved(pool.tensor_copy(gidx[par][:, :], ti[:, ds(col, 1)]), plain=True)
                        gather(par)
                    for par in range(2):
                        pool.wait_ge(ya_ready[l], 2 * it + (par + 2))
                        pool.wait_ge(yd_ready[l], 2 * it + (par + 2))
                        col = column(2 * it + par)
                        link.count.wait(y_out[l][par], 16 * it + 16, consts)
                        moved(pool.tensor_copy(sidx[par][:, :], td[:, ds(col, 1)]), plain=True)
                        scatter(par, yt[par])
                for par in range(2):
                    link.count.wait(xg_in[l][par], 16 * iters + 16, consts)
                    link.count.wait(y_out[l][par], 16 * iters + 16, consts)
                pool.memset(gidx[0][:, :], 0).then_inc(moe_done[l], 1)

            ln_shift(0)
            dispatch(0)
            ln_shift(1)
            pool.wait_ge(unit_done, U_WOUT2 + 2)
            link(pool.memset(qz[0][64:P, :, :], 0.0))
            link(pool.memset(qz[1][0:64, :, :], 0.0))
            pool.wait_ge(ev_d, 19 + 2)
            pool.wait_ge(ev_a, 17 + 2)

            def stage_q(hp, par):
                rr = slice(64 * par, 64 * par + 64)
                ins = pool.tensor_copy(qz[par][rr, :, :], q3[rr, :, ds(hp, 1), :].rearrange("p g a t -> p (g a) t"))
                ins.then_inc(qz_ready, 1)
                if isinstance(hp, int):
                    pool.wait_ge(qz_ready, 2 * hp + par + 1)
                else:
                    link.count.wait(qz_ready, 2 * hp + (par + 1), consts)
                pool.tensor_tensor(bh[par][:, :, :], near[:, :, :],
                                   nslope[:, None, ds(2 * hp + par, 1)].to_broadcast([P, 2, 256]), ALU.mult)\
                    .then_inc(bh_ready, 1)

            stage_q(0, 0)
            pool.wait_ge(bh_ready, 1)
            stage_q(0, 1)
            with pool.Fori(1, 4) as hp:
                for par in range(2):
                    pool.wait_ge(sb_ready, 4 * hp + (2 * par - 2))
                    pool.wait_ge(bh_ready, 2 * hp + par)
                    link.count.wait(s2_ready, 4 * hp + 2 * par, consts)
                    stage_q(hp, par)
            pool.wait_ge(wn_ready, 1)
            for hp in range(4):
                o2 = q3[:, 2, :, 2 * DH * hp:2 * DH * (hp + 1)].rearrange("p t (u c) -> p t u c", u=2)
                wb = w2[:, :, 2 * hp:2 * hp + 2, None].to_broadcast([P, NT, 2, DH])
                pool.tensor_tensor(o2, o2, wb, ALU.mult).then_inc(far_scaled, 1)
            ln_shift(2)
            dispatch(1)
            ln_shift(3)

        @block.scalar
        def _(act):
            link = Order(act, act_o)
            act.sem_inc(ev_a, 2)
            for l in range(2):
                act.sem_inc(xgt_a[l], 1)
                act.sem_inc(ya_ready[l], 1)
            act.sem_inc(d_ready, 2)
            gates = xe[:, GATE0:GATE0 + 8].rearrange("(k p) c -> p k c", p=P)
            act.dma_start(wif[:, :, :], gates).then_inc(gate_in, 16)
            act.dma_start(cwr[0:4, :], conv_w[0]).then_inc(cw_in, 16)
            act.dma_start(cwr[4:5, :], conv_b).then_inc(cw_in, 16)
            act.dma_start(gb[0:4, :], i_bias.rearrange("a h -> h a")).then_inc(gb_in, 16)
            act.dma_start(gb[32:36, :], f_bias.rearrange("a h -> h a")).then_inc(gb_in, 16)
            act.dma_start(gn[:, 0, :], mlstm_norm_g.to_broadcast([P, NH * HD])).then_inc(gn_in, 16)
            act.dma_start(gn[:, 1, :], ret_norm_g.to_broadcast([P, NH * HD])).then_inc(gn_in, 16)
            act.dma_start(rw[:, :, :], router_w.rearrange("(k p) e -> p k e", p=P)).then_inc(rw_in, 16)
            act.dma_start(rb[:, :], router_bias.rearrange("(a e) -> a e", a=1).to_broadcast([P, E]))\
               .then_inc(rw_in, 16)

            def split_xt(base, nk):
                for k in range(nk):
                    act.wait_ge(xt_ps, base + k + 1)
                    act.activation(xt_hi[:, k, :], bank[k][:, :], ACT.Copy).then_inc(xt_h, 1)

            def split_unit(u, slot):
                act.wait_ge(raw_in[slot], u * 8 + (16 - 8 * slot) if not isinstance(u, int)
                            else 16 * (u // 2 + 1))
                act.wait_ge(unit_done, u + 1)
                act.activation(wh[slot][:, :, :], raw[slot][:, :, :], ACT.Copy).then_inc(w_hi, 1)

            def evacuate(c, dsts, scale=1.0):
                act.wait_ge(unit_done, 2 * c + 4)
                for dst, src in dsts:
                    ins = act.activation(dst, src, ACT.Copy, scale=scale)
                ins.then_inc(ev_a, 1)

            act.wait_ge(gate_in, 16)
            act.activation(wif_hi[:, :, :], wif[:, :, :], ACT.Copy).then_inc(gate_hi, 1)
            split_xt(0, KT)
            for u in range(2):
                split_unit(u, u)
            act.wait_ge(gate_exp, 1)
            link(act.activation(ex[:, :], zf[:, :], ACT.Exp))
            act.activation(ex[:, :], ex[:, :], ACT.Ln, bias=one[0:4, 0:1]).then_inc(gate_ln, 1)
            with act.Fori(0, 2) as j:
                for i in range(4):
                    st = 4 * (i % 2)
                    split_unit(8 * j + (2 * i + 2), 0)
                    if i < 2:
                        dsts = [(qk[:, ds(j, 1), i, b, :].rearrange("p a t -> p (a t)"), bank[st + b][:, :])
                                for b in range(2)]
                    elif i == 2:
                        dsts = [(v[:, ds(j, 1), b, :, 0:HD].rearrange("p a h e -> p (a h) e"),
                                 bank[st + b][:, :].rearrange("p (h e) -> p h e", e=HD)) for b in range(2)]
                    else:
                        dsts = [(og[:, ds(j, 1), b, :].rearrange("p a t -> p (a t)"), bank[st + b][:, :])
                                for b in range(2)]
                    evacuate(4 * j + i, dsts)
                    split_unit(8 * j + (2 * i + 3), 1)
            act.wait_ge(ev_d, 8 + 2)
            act.wait_ge(ev_a, 8 + 2)
            act.activation(og[:, 1, :, :], og[:, 1, :, :], ACT.Silu).then_inc(og_act, 1)
            act.wait_ge(conv_done, 1)
            act.activation(qk[:, 0, :, :, :], qk[:, 0, :, :, :], ACT.Silu).then_inc(silu_done, 1)
            link(act.activation(og[:, 0, :, :], og[:, 0, :, :], ACT.Sigmoid))

            act.wait_ge(consts, 1)
            act.wait_ge(unit_done, 16 + 2)
            act.wait_ge(silu_done, 1)

            def stage_k(branch, hd, par, n):
                act.wait_ge(s_ready, n + 1)
                act.activation(ks[par][:, :], qk[:, branch, 1, ds(hd, 1), :].rearrange("p a t -> p (a t)"),
                               ACT.Copy, scale=SCALE).then_inc(ks_ready, 1)

            with act.Fori(0, 2) as i:
                for par in range(2):
                    stage_k(1, 2 * i + par, par, 2 * i + par)
                for par in range(2):
                    act.wait_ge(pt_ready, 2 * i + (par + 1))
                    act.activation(dd[par][:, 0:T], dist[:, :], ACT.Exp, scale=lgam[:, ds(2 * i + par, 1)])\
                       .then_inc(d_ready, 1)
            act.wait_ge(mb_ps, 1)
            for i in range(NH):
                ins = act.activation(mb[:, i, :], bank[i][:, :], ACT.Copy)
            ins.then_inc(mb_sb, 1)
            act.wait_ge(uc_sb, 1)
            act.activation(en[:, :, :], uc[:, :, 32:32 + NH], ACT.Exp).then_inc(en_sb, 1)
            act.wait_ge(mb_sb, 1)
            with act.Fori(0, 2) as i:
                for par in range(2):
                    stage_k(0, 2 * i + par, par, 2 * i + (NH + par))
                for par in range(2):
                    hd = 2 * i + par
                    act.wait_ge(pt_ready, 2 * i + (NH + par + 1))
                    act.wait_ge(mbd_ready, 2 * i + (par + 1))
                    for kb in range(NT):
                        u_s = uc[:, kb, ds(hd, 1)]
                        n = T - P * (kb + 1)
                        if n:
                            act.activation(dd[par][:, OFF[kb] + P:OFF[kb] + P + n],
                                           mb[:, ds(hd, 1), P * (kb + 1):T].rearrange("p a t -> p (a t)"),
                                           ACT.Exp, scale=-1.0, bias=u_s)
                        ins = act.activation(dd[par][:, OFF[kb]:OFF[kb] + P], mbd[par][:, kb, :],
                                             ACT.Exp, scale=-1.0, bias=u_s)
                    ins.then_inc(d_ready, 1)
            split_xt(8, KT)
            split_unit(U_WOUT + 2, 0)
            split_unit(U_WOUT + 3, 1)

            def ln_normalise(n):
                act.wait_ge(ln_nmr, n + 1)
                for t in range(NT):
                    act.activation(h[:, t, :], h[:, t, :], ACT.Identity, scale=rstd[:, t:t + 1],
                                   bias=nmr[:, t:t + 1]).then_inc(ln_norm, 1)

            def router(l):
                for t in range(NT):
                    act.wait_ge(rt_ps, NT * l + t + 1)
                    for b in range(2):
                        ins = act.activation(ht[:, 4 * b:4 * b + 4, t * P:(t + 1) * P],
                                             bank[2 * (t % 2) + b][:, :].rearrange("p (k t) -> p k t", t=P),
                                             ACT.Copy)
                    ins.then_inc(rt_sb, 1)
                act.wait_ge(lg_ps, l + 1)
                act.activation(aff[:, :, :], bank[4][:, 0:NT * E].rearrange("p (t e) -> p t e", e=E),
                               ACT.Sigmoid).then_inc(aff_ready, 1)

            def experts(l):
                act.wait_ge(tb_ready, l + 1)
                iters = act.value_load(ni[0:1, 1:2], min_val=1, max_val=NBLK // 4)

                def rows_t(q, par):
                    act.wait_ge(xg_tr[l], q + (par + 1))
                    act.wait_ge(gu_done[l], q + (par + 1))
                    act.activation(xgt[par][:, 0:4, :], bank[0][:, :].rearrange("p (k t) -> p k t", t=P),
                                   ACT.Copy).then_inc(xgt_a[l], 1)

                def silu(q, par):
                    act.wait_ge(gu_done[l], q + (par + 3))
                    act.wait_ge(hh_ready[l], q + (par + 1))
                    act.activation(sg[par][:, :], bank[2 + par][:, 0:F], ACT.Silu).then_inc(sg_ready[l], 1)

                def hidden_t(q, par):
                    act.wait_ge(ht_tr[l], q + (par + 3))
                    act.wait_ge(dn_done[l], q + (par + 1))
                    act.activation(htt[par][:, :, :], bank[4][:, 0:2 * P].rearrange("p (k t) -> p k t", t=P),
                                   ACT.Copy).then_inc(ht_sb[l], 1)

                def y_gated(q, par, it):
                    act.wait_ge(dn_done[l], q + (par + 3))
                    act.wait_ge(y_out[l][par], 16 * it + 16)
                    act.activation(yt[par][:, 0:512], bank[5][:, :], ACT.Copy,
                                   scale=gt[:, ds(q + par, 1)]).then_inc(ya_ready[l], 1)

                with act.Fori(0, iters) as it:
                    q = 2 * it
                    rows_t(q, 0)
                    silu(q, 0)
                    rows_t(q, 1)
                    hidden_t(q, 0)
                    y_gated(q, 0, it)
                    silu(q, 1)
                    hidden_t(q, 1)
                    y_gated(q, 1, it)

            ln_normalise(0)
            router(0)
            experts(0)
            ln_normalise(1)

            split_xt(16, KT)
            for u in range(2):
                split_unit(U_ODD + u, u)

            def odd_evac(c, st, dst, src_of, scale=1.0):
                evacuate(c, [(dst(b), src_of(bank[st + b][:, :])) for b in range(2)], scale)

            def q_scale(i):
                return 1.0 if i else DH ** -0.5

            for i, t in enumerate((q3, k3)):
                split_unit(U_ODD + 2 * i + 2, 0)
                odd_evac(10 + i, 4 * i, lambda b: t[:, 0, b, :], lambda s: s, q_scale(i))
                split_unit(U_ODD + 2 * i + 3, 1)
            with act.Fori(1, 3) as g:
                for i, t in enumerate((q3, k3)):
                    split_unit(4 * g + (U_ODD + 2 * i + 2), 0)
                    odd_evac(2 * g + (10 + i), 4 * i,
                             lambda b: t[:, ds(g, 1), b, :].rearrange("p g (a j) -> p (g a) j", a=4),
                             perm, q_scale(i))
                    split_unit(4 * g + (U_ODD + 2 * i + 3), 1)
            for g in range(3):
                split_unit(U_ODDV + 2 * g + 2, 0)
                odd_evac(16 + g, 4 * (g % 2), lambda b: v3[:, g, b, :], lambda s: s)
                split_unit(U_ODDV + 2 * g + 3, 1)

            def exps(hp, k):
                lay = k % 2
                act.wait_ge(nm_ready, 4 * hp + (k + 1))
                for t in range(NT):
                    cols = slice(P, 256) if (lay == 0 and t == 0) else slice(0, 256)
                    ins = act.activation(sc[lay][:, t, cols], sc[lay][:, t, cols], ACT.Exp,
                                         bias=nm[lay][:, t:t + 1],
                                         accum_out=dn[:, lay, t, ds(2 * hp + k // 2, 1)])
                ins.then_inc(p_ready, 1)

            def keep_weights(hp, k):
                lay = k % 2
                act.wait_ge(t_ready, 4 * hp + (k + 1))
                act.wait_ge(o2_ready, 4 * hp + (k + 1))
                lo = P if lay == 0 else 0
                act.activation(ptt[lay][:, 0:2, :].rearrange("p a c -> p (a c)")[:, lo:512],
                               bank[4][:, lo:512], ACT.Copy).then_inc(pta, 1)

            def pair_steps(hp, last):
                for k in range(4):
                    if not (last and k == 3):
                        exps(hp, k + 1)
                    keep_weights(hp, k)

            exps(0, 0)
            with act.Fori(0, 3) as hp:
                pair_steps(hp, False)
            pair_steps(3, True)
            act.wait_ge(mx_ready, 1)
            link(act.activation(w1[:, :, :], w1[:, :, :], ACT.Exp))
            act.activation(w2[:, :, :], w2[:, :, :], ACT.Exp).then_inc(we_ready, 1)
            split_xt(24, 4)
            ln_normalise(2)
            router(1)
            experts(1)
            ln_normalise(3)

        @block.vector
        def _(dve):
            link = Order(dve, dve_o)
            dve.sem_inc(w_lo, 2)
            dve.sem_inc(ev_d, 2)
            dve.sem_inc(pt_ready, 2)
            dve.sem_inc(o_read, 2)
            dve.sem_inc(oe_ready, 2)
            for l in range(2):
                dve.sem_inc(xgt_d[l], 1)
                dve.sem_inc(yd_ready[l], 1)
                dve.sem_inc(hh_ready[l], 2)

            def split_xt(base, nk):
                for k in range(nk):
                    dve.wait_ge(xt_h, base + k + 1)
                    dve.tensor_tensor(xt_lo[:, k, :], bank[k][:, :], xt_hi[:, k, :], ALU.subtract)\
                       .then_inc(xt_l, 1)

            def split_unit(u, slot):
                dve.wait_ge(w_hi, u + 1)
                dve.tensor_tensor(wl[slot][:, :, :], raw[slot][:, :, :], wh[slot][:, :, :], ALU.subtract)\
                   .then_inc(w_lo, 1)

            def evacuate(c, dsts, scale=None):
                dve.wait_ge(unit_done, 2 * c + 4)
                for dst, src in dsts:
                    ins = (dve.tensor_scalar(dst, src, scale, None, ALU.mult) if scale
                           else dve.tensor_copy(dst, src))
                ins.then_inc(ev_d, 1)

            def rsqrt(var, n):
                y, w, s = rstd[:, 0:n], nwt[:, 0:n], nmr[:, 0:n]
                link(dve.tensor_scalar(s, var, EPS, None, ALU.add))
                link(dve.tensor_scalar(y.bitcast(i32), s.bitcast(i32), -0.5, 1597463007.0, ALU.mult, ALU.add))
                for _ in range(3):
                    link(dve.scalar_tensor_tensor(w, y, -0.5, y, ALU.mult, ALU.mult))
                    link(dve.tensor_tensor(w, w, s, ALU.mult))
                    link(dve.scalar_tensor_tensor(y, w, 1.5, y, ALU.add, ALU.mult))

            dve.wait_ge(consts, 1)
            quarter, rest = hm[1][:, 0, :], hm[1][:, 1, :]
            link(dve.tensor_scalar(quarter.bitcast(i32), jdiff[:, :], 2, None, ALU.arith_shift_right))
            link(dve.tensor_copy(rest, quarter.bitcast(i32)))
            link(dve.tensor_copy(quarter, jdiff[:, :]))
            link(dve.scalar_tensor_tensor(rest, rest, -4.0, quarter, ALU.mult, ALU.add))
            link(dve.scalar_tensor_tensor(near[:, 1, P:2 * P], rest, BIG, near[:, 1, P:2 * P], ALU.mult, ALU.add))
            dve.wait_ge(gate_hi, 1)
            dve.tensor_tensor(wif_lo[:, :, :], wif[:, :, :], wif_hi[:, :, :], ALU.subtract).then_inc(gate_lo, 1)
            split_xt(0, KT)
            for u in range(2):
                split_unit(u, u)
            dve.wait_ge(cw_ps, 1)
            dve.tensor_copy(cw[:, :, :], bank[6][:, 0:40].rearrange("p (k c) -> p k c", c=5)).then_inc(cw_sb, 1)
            dve.wait_ge(gate_ps, 1)
            dve.wait_ge(consts, 1)
            logits = bank[4][:, 0:32].rearrange("p (t c) -> p t c", c=8)
            dve.tensor_copy(g64[:, :, 0:4], logits[:, :, 0:4])
            dve.tensor_copy(g64[:, :, 32:36], logits[:, :, 4:8]).then_inc(gate_sb, 1)
            dve.wait_ge(gate_tr, 1)
            dve.wait_ge(gb_in, 32)
            fbias = gb[32:36, 0:1]
            link(dve.tensor_scalar(zf[:, :], bank[7][32:36, :], fbias, None, ALU.add))
            link(dve.tensor_copy(mrow[:, :], zf[:, :]))
            dve.scalar_tensor_tensor(zf[:, :], mrow[:, :], -1.0, mrow[:, :], ALU.mult, ALU.min)\
               .then_inc(gate_exp, 1)
            dve.wait_ge(gate_ln, 1)
            link(dve.scalar_tensor_tensor(zf[:, :], mrow[:, :], 0.0, ex[:, :], ALU.min, ALU.subtract))
            link(dve.memset(ex[:, :], 1.0))
            link(dve.tensor_tensor_scan(mrow[:, :], ex[:, :], zf[:, :], 0.0, ALU.mult, ALU.add))
            link(dve.scalar_tensor_tensor(rows[0:4, :], bank[7][0:4, :], gb[0:4, 0:1], mrow[:, :],
                                          ALU.add, ALU.subtract))
            link(dve.tensor_copy(zf[:, :], mrow[:, :]))
            link(dve.tensor_tensor_scan(mrow[:, :], rows[0:4, :], rows[0:4, :], 0.0, ALU.max, ALU.max))
            dve.scalar_tensor_tensor(rows[32:36, :], zf[:, :], -1.0, mrow[:, :], ALU.mult, ALU.subtract)\
               .then_inc(rows_ready, 1)

            with dve.Fori(0, 2) as j:
                for i in range(4):
                    st = 4 * (i % 2)
                    split_unit(8 * j + (2 * i + 2), 0)
                    if i < 2:
                        dsts = [(qk[:, ds(j, 1), i, b, :].rearrange("p a t -> p (a t)"), bank[st + b][:, :])
                                for b in (2, 3)]
                    elif i == 2:
                        dsts = [(v[:, ds(j, 1), b, :, 0:HD].rearrange("p a h e -> p (a h) e"),
                                 bank[st + b][:, :].rearrange("p (h e) -> p h e", e=HD)) for b in (2, 3)]
                    else:
                        dsts = [(og[:, ds(j, 1), b, :].rearrange("p a t -> p (a t)"), bank[st + b][:, :])
                                for b in (2, 3)]
                    evacuate(4 * j + i, dsts)
                    split_unit(8 * j + (2 * i + 3), 1)
            dve.wait_ge(uc_ps, 1)
            dve.tensor_copy(uc[:, :, :], bank[4][:, 0:256].rearrange("p (t c) -> p t c", c=64)).then_inc(uc_sb, 1)

            def weigh(par, n, dec):
                dve.wait_ge(s_ready, n + (par + 3))
                dve.wait_ge(d_ready, n + (par + 3))
                dve.wait_ge(o_ready, n + (par + 1))
                b = 3 * par
                src = (bank[b][:, :], bank[b + 1][:, 0:384], bank[b + 2][:, 0:256], bank[b + 1][:, 384:512])
                for kb in range(NT):
                    w = T - P * kb
                    ins = dve.tensor_tensor(pt[par][:, OFF[kb]:OFF[kb] + w], src[kb], dec(par, kb, w), ALU.mult)
                ins.then_inc(pt_ready, 1)

            def head_stats(src_of, par):
                for t in range(NT):
                    ins = dve.bn_stats(stat[:, 4 * par + t, :], src_of(t))
                link(ins, plain=True)
                for t in range(NT):
                    ins = dve.bn_aggr(mv[:, 4 * par + t, :], stat[:, 4 * par + t, :])
                link(ins)

            def head_normalise(src_of, par):
                for t in range(NT):
                    c = 4 * par + t
                    ins = dve.tensor_scalar(hm[par][:, t, :], src_of(t), mv[:, c, 0:1], rstd[:, c:c + 1],
                                            ALU.subtract, ALU.mult)
                return ins

            dve.wait_ge(og_ready, 1)
            with dve.Fori(0, 2) as i, link.rolled(i, 2 + 2 + 11 + 2, 2):
                for par in range(2):
                    weigh(par, 2 * i, lambda par, kb, w: dd[par][:, 0:w])
                o = [lambda t, p=par: bank[6 + p][:, t * HD:(t + 1) * HD] for par in range(2)]
                for par in range(2):
                    dve.wait_ge(o_ready, 2 * i + (par + 3))
                    head_stats(o[par], par)
                rsqrt(mv[:, :, 1], 8)
                for par in range(2):
                    dve.wait_ge(y_done, 2 * i + (par + 1))
                    link(head_normalise(o[par], par))
                    dve.tensor_copy(nwt[:, 0:1], rstd[:, 0:1]).then_inc(o_read, 1)
                    dve.tensor_copy(nwt[:, 1:2], rstd[:, 0:1]).then_inc(yn_ready, 1)
            dve.wait_ge(en_sb, 1)
            with dve.Fori(0, 2) as i, link.rolled(i, 2 * 5 + 4 + 11 + 2, 2):
                for par in range(2):
                    weigh(par, 2 * i + NH, lambda par, kb, w: dd[par][:, OFF[kb]:OFF[kb] + w])
                for par in range(2):
                    hd = 2 * i + par
                    dve.wait_ge(o_ready, 2 * i + (NH + par + 3))
                    dve.wait_ge(y_done, 2 * i + (NH + par + 1))
                    ob = [bank[6 + b][:, 0:2 * VW].rearrange("p (t c) -> p t c", c=VW) for b in range(2)]
                    for b in range(2):
                        ins = dve.tensor_copy(nmr[:, 2 * b:2 * b + 2], ob[b][:, :, HD])
                    link(ins)
                    link(dve.scalar_tensor_tensor(nwt[:, 0:4], nmr[:, 0:4], -1.0, nmr[:, 0:4], ALU.mult, ALU.max))
                    link(dve.tensor_tensor(nwt[:, 0:4], nwt[:, 0:4],
                                           en[:, :, ds(hd, 1)].rearrange("p t a -> p (t a)"), ALU.max))
                    link(dve.reciprocal(nwt[:, 0:4], nwt[:, 0:4]))
                    for t in range(NT):
                        ins = dve.scalar_tensor_tensor(hm[par][:, t, :], ob[t // 2][:, t % 2, 0:HD], nwt[:, t:t + 1],
                                                       og[:, 0, t, ds(hd * HD, HD)], ALU.mult, ALU.mult)
                    link(ins)
                    dve.tensor_copy(nmr[:, 4:5], nwt[:, 0:1]).then_inc(o_read, 1)
                    head_stats(lambda t, p=par: hm[p][:, t, :], par)
                rsqrt(mv[:, :, 1], 8)
                for par in range(2):
                    link(head_normalise(lambda t, p=par: hm[p][:, t, :], par))
                    dve.tensor_copy(nwt[:, par:par + 1], rstd[:, 0:1]).then_inc(yn_ready, 1)

            def residual(c, half):
                dve.wait_ge(unit_done, c)
                st = 4 * (half if c < 30 else 1 - half)
                for t in range(NT):
                    hs = h[:, t, half * C:(half + 1) * C]
                    ins = dve.scalar_tensor_tensor(hs, hs, ALPHA, bank[st + t][:, :], ALU.mult, ALU.add)
                ins.then_inc(ev_d, 1)
                return ins

            def layer_norm(n):
                for t in range(NT):
                    for s in range(2):
                        ins = dve.bn_stats(stat[:, 2 * t + s, :], h[:, t, s * 512:(s + 1) * 512])
                link(ins)
                for t in range(NT):
                    ins = dve.bn_aggr(mv[:, t, :], stat[:, 2 * t:2 * t + 2, :])
                link(ins)
                rsqrt(mv[:, 0:NT, 1], NT)
                dve.scalar_tensor_tensor(nmr[:, 0:NT], mv[:, 0:NT, 0], -1.0, rstd[:, 0:NT], ALU.mult, ALU.mult)\
                   .then_inc(ln_nmr, 1)
                dve.wait_ge(ln_in, 32 * (n + 1))
                for t in range(NT):
                    dve.wait_ge(ln_norm, 4 * n + t + 1)
                    dve.tensor_tensor(h[:, t, :], h[:, t, :], lngb[:, 0, :], ALU.mult).then_inc(ln_scaled, 1)

            def route(l):
                row = lambda n: row128[:, 0:n]
                link(dve.memset(gs[:, :, :], -BIG))
                dve.wait_ge(aff_ready, l + 1)
                dve.wait_ge(rw_in, 32)
                link(dve.tensor_tensor(sel[:, :, :], aff[:, :, :], rb[:, None, :].to_broadcast([P, NT, E]), ALU.add))
                for t in range(NT):
                    for g in range(E // EG):
                        ins = dve.max(m8g[:, t, g, :], sel[:, t, EG * g:EG * (g + 1)])
                link(ins)
                link(dve.tensor_tensor(gs[:, :, 0:4], m8g[:, :, :, 0], m8g[:, :, :, 1], ALU.add))
                for t in range(NT):
                    ins = dve.max(gm[:, t, :], gs[:, t, :])
                link(ins)
                for t in range(NT):
                    ins = dve.max_index(gi[:, t, :], gm[:, t, :], gs[:, t, :])
                link(ins)
                link(dve.tensor_copy(gif[:, :], gi[:, :, 0]))
                link(dve.tensor_tensor(pen[:, :, :], row(4)[:, None, :].to_broadcast([P, NT, 4]),
                                       gif[:, :, None].to_broadcast([P, NT, 4]), ALU.is_equal))
                link(dve.tensor_scalar(pen[:, :, :], pen[:, :, :], 1.0, BIG, ALU.subtract, ALU.mult))
                link(dve.tensor_tensor(msel[:, :, :].rearrange("p t (g e) -> p t g e", e=EG),
                                       sel[:, :, :].rearrange("p t (g e) -> p t g e", e=EG),
                                       pen[:, :, :, None].to_broadcast([P, NT, 4, EG]), ALU.add))
                for t in range(NT):
                    ins = dve.max(v8[:, t, :], msel[:, t, :])
                link(ins)
                for t in range(NT):
                    ins = dve.max_index(i8[:, t, :], v8[:, t, :], msel[:, t, :])
                link(ins)
                link(dve.tensor_copy(ef[:, :, :], i8[:, :, 0:2].rearrange("p t c -> p c t")))
                for c in range(2):
                    ins = dve.tensor_tensor(oh[:, c, :, :], row(E)[:, None, :].to_broadcast([P, NT, E]),
                                            ef[:, c, :, None].to_broadcast([P, NT, E]), ALU.is_equal)
                link(ins)
                dve.tensor_tensor(ohs[:, :, :], oh[:, 0, :, :], oh[:, 1, :, :], ALU.add).then_inc(oh_ready, 1)
                for c in range(2):
                    ins = dve.tensor_tensor(t1[:, c, :, :], oh[:, c, :, :], aff[:, :, :], ALU.mult)
                link(ins)
                link(dve.tensor_reduce(ga[:, :, :], t1[:, :, :, :], AX.X, ALU.add))
                link(dve.tensor_tensor(gd[:, :], ga[:, 0, :], ga[:, 1, :], ALU.add))
                link(dve.reciprocal(gd[:, :], gd[:, :]))
                link(dve.tensor_tensor(ga[:, :, :], ga[:, :, :], gd[:, None, :].to_broadcast([P, 2, NT]), ALU.mult))
                dve.wait_ge(cnt_ps, l + 1)
                link(dve.tensor_tensor(cm[:, :, :], bank[5][:, P:P + E, None].to_broadcast([P, E, 8]),
                                       thr[:, None, :].to_broadcast([P, E, 8]), ALU.is_gt))
                link(dve.tensor_reduce(nb[:, :], cm[:, :, :], AX.X, ALU.add))
                link(dve.tensor_tensor_scan(bend[:, :], one[:, 0:1].to_broadcast([P, E]), nb[:, :], 0.0,
                                            ALU.mult, ALU.add))
                link(dve.tensor_tensor(cmp[0:1, :, :], bend[0:1, None, :].to_broadcast([1, NBLK, E]),
                                       row(NBLK)[0:1, :, None].to_broadcast([1, NBLK, E]), ALU.is_le))
                link(dve.tensor_reduce(ber[0:1, :], cmp[0:1, :, :], AX.X, ALU.add))
                link(dve.tensor_scalar(be[0:1, :], ber[0:1, :], float(E - 1), None, ALU.min))
                link(dve.tensor_scalar(ni[0:1, 0:1], bend[0:1, E - 1:E], 3.0, None, ALU.add))
                link(dve.tensor_tensor(cmp[0:1, 0, 0:4], ber[0:1, 0:4], row(4)[0:1, :], ALU.not_equal))
                link(dve.tensor_reduce(ni[0:1, 2:3], cmp[0:1, 0, 0:4], AX.X, ALU.max))
                dve.tensor_scalar(ni[0:1, 1:2], ni[0:1, 0:1], 2, None, ALU.arith_shift_right).then_inc(blk_ready, 1)
                link(dve.tensor_tensor(bst[:, :], bend[:, :], nb[:, :], ALU.subtract))
                link(dve.tensor_scalar(bst[:, :], bst[:, :], float(B), None, ALU.mult))
                link(dve.tensor_tensor(pos[:, :, :], bank[5][:, 0:NT * E].rearrange("p (t e) -> p t e", e=E),
                                       bst[:, None, :].to_broadcast([P, NT, E]), ALU.add))
                for c in range(2):
                    ins = dve.tensor_tensor(t1[:, c, :, :], oh[:, c, :, :], pos[:, :, :], ALU.mult)
                link(ins)
                link(dve.tensor_reduce(dest[:, :], t1[:, :, :, :].rearrange("p c t e -> p (c t) e"), AX.X, ALU.add))
                link(dve.tensor_copy(di[:, :], dest[:, :]))
                link(dve.tensor_scalar(di[:, :], di[:, :], 7, None, ALU.arith_shift_right))
                link(dve.tensor_copy(pf[:, :], di[:, :]))
                link(dve.scalar_tensor_tensor(rm[:, :], pf[:, :], -float(P), dest[:, :], ALU.mult, ALU.add))
                link(dve.tensor_tensor(aoh[:, :, :], row(P)[:, None, :].to_broadcast([P, 8, P]),
                                       rm[:, :, None].to_broadcast([P, 8, P]), ALU.is_equal))
                link(dve.tensor_tensor(eq[:, :, :], row(NCOL)[:, None, :].to_broadcast([P, 8, NCOL]),
                                       pf[:, :, None].to_broadcast([P, 8, NCOL]), ALU.is_equal))
                for n, val in enumerate((tok_of, dst_of, ga)):
                    ins = dve.tensor_tensor(
                        bv[:, :, n * NCOL:(n + 1) * NCOL], eq[:, :, :],
                        val[:, :, :].rearrange("p c t -> p (c t)")[:, :, None].to_broadcast([P, 8, NCOL]), ALU.mult)
                ins.then_inc(ab_ready, 1)
                dve.wait_ge(tb_ps, l + 1)
                tb = bank[6]
                dve.tensor_scalar(ti[:, :], tb[:, 0:NCOL], float(EMPTY), None, ALU.add)
                dve.tensor_scalar(td[:, :], tb[:, NCOL:2 * NCOL], float(EMPTY), None, ALU.add)
                dve.tensor_copy(gt[:, :], tb[:, 2 * NCOL:3 * NCOL]).then_inc(tb_ready, 1)

            def experts(l):
                dve.wait_ge(tb_ready, l + 1)
                iters = dve.value_load(ni[0:1, 1:2], min_val=1, max_val=NBLK // 4)

                def rows_t(q, par):
                    dve.wait_ge(xg_tr[l], q + (par + 1))
                    dve.wait_ge(gu_done[l], q + (par + 1))
                    dve.tensor_copy(xgt[par][:, 4:8, :], bank[1][:, :].rearrange("p (k t) -> p k t", t=P))\
                       .then_inc(xgt_d[l], 1)

                def hidden(q, par):
                    dve.wait_ge(sg_ready[l], q + (par + 1))
                    dve.wait_ge(ht_tr[l], q + (par + 1))
                    dve.tensor_tensor(hh[par][:, :], sg[par][:, :], bank[2 + par][:, F:2 * F], ALU.mult)\
                       .then_inc(hh_ready[l], 1)

                def y_gated(q, par, it):
                    dve.wait_ge(dn_done[l], q + (par + 3))
                    dve.wait_ge(y_out[l][par], 16 * it + 16)
                    dve.tensor_scalar(yt[par][:, 512:D], bank[6][:, :], gt[:, ds(q + par, 1)], None, ALU.mult)\
                       .then_inc(yd_ready[l], 1)

                with dve.Fori(0, iters) as it:
                    q = 2 * it
                    rows_t(q, 0)
                    hidden(q, 0)
                    rows_t(q, 1)
                    y_gated(q, 0, it)
                    hidden(q, 1)
                    y_gated(q, 1, it)

            def add_experts(l):
                dve.wait_ge(h_stored, 16 * NT * (l + 1))
                for t in range(NT):
                    dve.wait_ge(y2_in[t % 2], 16 * (2 * l + t // 2 + 1))
                    yy = y2[t % 2]
                    link(dve.scalar_tensor_tensor(h[:, t, :], h[:, t, :], ALPHA, yy[:, 0:D], ALU.mult, ALU.add))
                    dve.tensor_tensor(h[:, t, :], h[:, t, :], yy[:, D:2 * D], ALU.add).then_inc(y2_read, 1)
                dve.wait_ge(y2_read, NT * (l + 1))

            split_xt(8, KT)
            split_unit(U_WOUT + 2, 0)
            split_unit(U_WOUT + 3, 1)
            residual(U_WOUT + 4, 0)
            residual(U_WOUT + 6, 1)
            dve.wait_ge(ev_d, 10 + 2)
            layer_norm(0)
            route(0)
            experts(0)
            add_experts(0)
            layer_norm(1)

            split_xt(16, KT)
            for u in range(2):
                split_unit(U_ODD + u, u)

            def odd_evac(c, st, dst, src_of, scale=None):
                evacuate(c, [(dst(b), src_of(bank[st + b][:, :])) for b in (2, 3)], scale)

            def q_scale(i):
                return None if i else DH ** -0.5

            for i, t in enumerate((q3, k3)):
                split_unit(U_ODD + 2 * i + 2, 0)
                odd_evac(10 + i, 4 * i, lambda b: t[:, 0, b, :], lambda s: s, q_scale(i))
                split_unit(U_ODD + 2 * i + 3, 1)
            with dve.Fori(1, 3) as g:
                for i, t in enumerate((q3, k3)):
                    split_unit(4 * g + (U_ODD + 2 * i + 2), 0)
                    odd_evac(2 * g + (10 + i), 4 * i,
                             lambda b: t[:, ds(g, 1), b, :].rearrange("p g (a j) -> p (g a) j", a=4),
                             perm, q_scale(i))
                    split_unit(4 * g + (U_ODD + 2 * i + 3), 1)
            for g in range(3):
                split_unit(U_ODDV + 2 * g + 2, 0)
                odd_evac(16 + g, 4 * (g % 2), lambda b: v3[:, g, b, :], lambda s: s)
                split_unit(U_ODDV + 2 * g + 3, 1)

            dve.wait_ge(unit_done, U_WOUT2 + 2)

            def biased(hp, k):
                lay, hd = k % 2, 2 * hp + k // 2
                if lay == 0:
                    dve.wait_ge(bh_ready, hd + 1)
                if isinstance(hp, int):
                    dve.wait_ge(s2_ready, 4 * hp + k + 3)
                else:
                    link.count.wait(s2_ready, 4 * hp + (k + 3), consts)
                for t in range(NT):
                    c = slice(P, 256) if (lay == 0 and t == 0) else slice(0, 256)
                    bk = bank[2 * lay + t // 2][:, 256 * (t % 2):256 * (t % 2) + 256]
                    ins = dve.tensor_tensor_reduce(out=sc[lay][:, t, c], in0=bk[:, c], in1=bh[k // 2 % 2][:, lay, c],
                                                   scale=1.0, scalar=-3.0e38, op0=ALU.add, op1=ALU.max,
                                                   accum_out=mm[lay][:, t:t + 1])
                link(ins)
                dve.tensor_scalar(nm[lay][:, :], mm[lay][:, :], -1.0, None, ALU.mult).then_inc(nm_ready, 1)
                dve.tensor_copy(ms[:, lay, :, ds(hd, 1)].rearrange("p t a -> p (t a)"), mm[lay][:, :])\
                   .then_inc(sb_ready, 1)

            def keep_weights(hp, k):
                dve.wait_ge(t_ready, 4 * hp + (k + 1))
                dve.wait_ge(o2_ready, 4 * hp + (k + 1))
                dve.tensor_copy(ptt[k % 2][:, 2:4, :].rearrange("p a c -> p (a c)"), bank[5][:, :])\
                   .then_inc(ptd, 1)

            def keep_out(hp, k):
                par, lay = k // 2, k % 2
                dve.wait_ge(o2_ready, 4 * hp + (k + 3))
                dve.wait_ge(qz_ready, 2 * hp + 2)
                dve.tensor_copy(
                    q3[:, lay, ds(hp, 1), :].rearrange("p g (t u c) -> p (g t) u c", t=NT, u=2)[:, :, par, :],
                    bank[6 + lay][:, 0:NT * DH].rearrange("p (t c) -> p t c", c=DH)).then_inc(oe_ready, 1)

            def pair_steps(hp, last):
                for k in range(4):
                    if not (last and k == 3):
                        biased(hp, k + 1)
                    keep_weights(hp, k)
                    if k:
                        keep_out(hp, k - 1)
                keep_out(hp, 3)

            biased(0, 0)
            with dve.Fori(0, 3) as hp, link.rolled(hp, 4, 3):
                pair_steps(hp, False)
            pair_steps(3, True)

            dve.wait_ge(far_in, 32)
            m1, d1, m2, d2 = ms[:, 0, :, :], dn[:, 0, :, :], me[:, :, 0:8], me[:, :, 8:16]
            dve.wait_ge(p_ready, 16)
            link(dve.tensor_tensor(mx[:, :, :], m1, m2, ALU.max))
            link(dve.tensor_tensor(w1[:, :, :], m1, mx[:, :, :], ALU.subtract))
            dve.tensor_tensor(w2[:, :, :], m2, mx[:, :, :], ALU.subtract).then_inc(mx_ready, 1)
            dve.wait_ge(we_ready, 1)
            link(dve.tensor_tensor(dsum[:, :, :], w1[:, :, :], d1, ALU.mult))
            link(dve.tensor_tensor(mx[:, :, :], w2[:, :, :], d2, ALU.mult))
            link(dve.tensor_tensor(dsum[:, :, :], dsum[:, :, :], mx[:, :, :], ALU.add))
            link(dve.reciprocal(dsum[:, :, :], dsum[:, :, :]))
            link(dve.tensor_tensor(w1[:, :, :], w1[:, :, :], dsum[:, :, :], ALU.mult))
            dve.tensor_tensor(w2[:, :, :], w2[:, :, :], dsum[:, :, :], ALU.mult).then_inc(wn_ready, 1)

            def near_out(hp):
                return q3[:, 0, hp, :].rearrange("p (t u c) -> p t u c", t=NT, u=2)

            for hp in range(4):
                ins = dve.tensor_tensor(near_out(hp), near_out(hp),
                                        w1[:, :, 2 * hp:2 * hp + 2, None].to_broadcast([P, NT, 2, DH]), ALU.mult)
            link(ins)
            for hp in range(4):
                dve.wait_ge(far_scaled, hp + 1)
                o2 = q3[:, 2, :, 2 * DH * hp:2 * DH * (hp + 1)].rearrange("p t (u c) -> p t u c", u=2)
                dve.tensor_tensor(near_out(hp), near_out(hp), o2, ALU.add).then_inc(yo_ready, 1)
            split_xt(24, 4)
            residual(U_WOUT2 + 1 + 2, 0)
            residual(U_WOUT2 + 2 + 2, 1)
            dve.wait_ge(ev_d, 21 + 2)
            layer_norm(2)
            route(1)
            experts(1)
            add_experts(1)
            layer_norm(3)

        @block.tensor
        def _(pe):
            pe.sem_inc(unit_done, 2)
            pe.sem_inc(s_ready, 2)
            pe.sem_inc(o_ready, 2)
            pe.sem_inc(s2_ready, 2)
            pe.sem_inc(o2_ready, 2)
            for l in range(2):
                pe.sem_inc(gu_done[l], 2)
                pe.sem_inc(dn_done[l], 2)
                pe.sem_inc(ht_tr[l], 2)

            def transpose_tiles(nk, src):
                for k in range(nk):
                    for t in range(NT):
                        ins = pe.transpose(bank[k][:, t * P:(t + 1) * P], src(k, t), ident[:, :])
                    ins.then_inc(xt_ps, 1)

            def unit(u, slot, half, out_of, x_cols=None, nk=8):
                pe.wait_ge(w_lo, u + 3)
                for i in range(4):
                    for kk in range(4):
                        k = 4 * half + kk
                        for n, (xp, wp) in enumerate(((xt_hi, wh), (xt_hi, wl), (xt_lo, wh))):
                            if x_cols is None:
                                a, b = wp[slot][:, kk, i * P:(i + 1) * P], xp[:, k, :]
                            else:
                                a, b = x_cols(xp, k, i), wp[slot][:, kk, :]
                            ins = pe.matmul(out_of(i), a, b, start=(k == 0 and n == 0),
                                            stop=(k == nk - 1 and n == 2))
                ins.then_inc(unit_done, 1)

            def in_order(xp, k, i):
                return xp[:, k, i * P:(i + 1) * P]

            def by_residue(xp, k, i):
                return perm(xp[:, k, :])[:, i, :]

            def chunk(c, a, u, st, x_cols=None):
                pe.wait_ge(ev_d, c + 1)
                if a is not None:
                    pe.wait_ge(ev_a, a + 1)
                for half in range(2):
                    unit(u + half, half, half, lambda i: bank[st + i][:, :], x_cols)

            pe.wait_ge(consts, 1)
            pe.wait_ge(x_in, 16)
            transpose_tiles(KT, lambda k, t: h[:, t, k * P:(k + 1) * P])
            pe.wait_ge(cw_in, 32)
            pe.wait_ge(xt_l, KT)
            for k in range(8):
                ins = pe.transpose(bank[6][:, 5 * k:5 * k + 5], cwr[0:5, k * P:(k + 1) * P], ident[0:5, 0:5])
            ins.then_inc(cw_ps, 1)
            pe.wait_ge(gate_lo, 1)
            for t in range(NT):
                for k in range(KT):
                    for n, (xp, wp) in enumerate(((xt_hi, wif_hi), (xt_hi, wif_lo), (xt_lo, wif_hi))):
                        ins = pe.matmul(bank[4][:, 8 * t:8 * t + 8], in_order(xp, k, t), wp[:, k, :],
                                        start=(k == 0 and n == 0), stop=(k == KT - 1 and n == 2))
            ins.then_inc(gate_ps, 1)
            pe.wait_ge(gate_sb, 1)
            for t in range(NT):
                ins = pe.transpose(bank[7][0:64, t * P:(t + 1) * P], g64[:, t, :], ident[:, :])
            ins.then_inc(gate_tr, 1)

            with pe.Fori(0, 2) as j:
                chunk(4 * j, 4 * j, 8 * j, 0)
                pe.wait_ge(rows_ready, 1)
                pe.wait_ge(cw_sb, 1)
                chunk(4 * j + 1, 4 * j + 1, 8 * j + 2, 4)
                chunk(4 * j + 2, 4 * j + 2, 8 * j + 4, 0, in_order)
                chunk(4 * j + 3, 4 * j + 3, 8 * j + 6, 4, in_order)

            pe.wait_ge(ev_a, 8 + 2)
            pe.wait_ge(ev_d, 8 + 2)
            for t in range(NT):
                ins = pe.transpose(bank[4][:, 64 * t:64 * t + 64], rows[:, t * P:(t + 1) * P], ident[0:64, 0:64])
            ins.then_inc(uc_ps, 1)
            pe.wait_ge(uc_sb, 1)

            def scores(branch, hd, par, n):
                pe.wait_ge(ks_ready, n + (par + 1))
                pe.wait_ge(pt_ready, n + (par + 1))
                b = 3 * par
                dst = (bank[b][:, :], bank[b + 1][:, 0:384], bank[b + 2][:, 0:256], bank[b + 1][:, 384:512])
                for kb in range(NT):
                    ins = pe.matmul(dst[kb], ks[par][:, kb * P:(kb + 1) * P],
                                    qk[:, branch, 0, ds(hd, 1), kb * P:T].rearrange("p a t -> p (a t)"),
                                    start=True, stop=True)
                ins.then_inc(s_ready, 1)

            def mix(branch, hd, par, n, width, dst, free):
                pe.wait_ge(pt_ready, n + (par + 3))
                pe.wait_ge(o_read, n + free)
                for t in range(NT):
                    for kb in range(t + 1):
                        c = OFF[kb] + (t - kb) * P
                        ins = pe.matmul(dst(t), pt[par][:, c:c + P],
                                        v[:, branch, kb, ds(hd, 1), 0:width].rearrange("p a e -> p (a e)"),
                                        start=(kb == 0), stop=(kb == t))
                ins.then_inc(o_ready, 1)

            with pe.Fori(0, 2) as i:
                for par in range(2):
                    scores(1, 2 * i + par, par, 2 * i)
                for par in range(2):
                    mix(1, 2 * i + par, par, 2 * i, HD,
                        lambda t: bank[6 + par][:, t * HD:(t + 1) * HD], par + 1)
            pe.wait_ge(pt_ready, NH + 2)
            for i in range(NH):
                ins = pe.matmul(bank[i][:, :], sel4[0:4, i, :], mrow[0:4, :], start=True, stop=True)
            ins.then_inc(mb_ps, 1)
            pe.wait_ge(mb_sb, 1)
            with pe.Fori(0, 2) as i:
                for par in range(2):
                    scores(0, 2 * i + par, par, 2 * i + NH)
                for par in range(2):
                    mix(0, 2 * i + par, par, 2 * i + NH, VW,
                        lambda t: bank[6 + t // 2][:, (t % 2) * VW:(t % 2 + 1) * VW], par + 2)

            pe.wait_ge(y_done, 8 + 2)
            pe.wait_ge(o_read, 8 + 2)
            transpose_tiles(KT, lambda k, t: og[:, k // 4, t, (k % 4) * HD:(k % 4 + 1) * HD])
            pe.wait_ge(xt_l, 2 * KT)
            chunk(8, None, U_WOUT, 0, in_order)
            chunk(9, None, U_WOUT + 2, 4, in_order)

            def router(l):
                for t in range(NT):
                    pe.wait_ge(ln_out, 8 * l + t + 1)
                    if t >= 2:
                        pe.wait_ge(rt_sb, NT * l + t - 1)
                    for k in range(KT):
                        ins = pe.transpose(bank[2 * (t % 2) + k // 4][:, (k % 4) * P:(k % 4 + 1) * P],
                                           h[:, t, k * P:(k + 1) * P], ident[:, :])
                    ins.then_inc(rt_ps, 1)
                for t in range(NT):
                    pe.wait_ge(rt_sb, NT * l + t + 1)
                    pe.wait_ge(rw_in, 32)
                    for k in range(KT):
                        ins = pe.matmul(bank[4][:, t * E:(t + 1) * E], ht[:, k, t * P:(t + 1) * P], rw[:, k, :],
                                        start=(k == 0), stop=(k == KT - 1))
                ins.then_inc(lg_ps, 1)
                pe.wait_ge(oh_ready, l + 1)
                for t in range(NT):
                    for s in range(t + 1):
                        ins = pe.matmul(bank[5][:, t * E:(t + 1) * E], (before if s == t else ones_bf)[:, :],
                                        ohs[:, s, :], start=(s == 0), stop=(s == t))
                for s in range(NT):
                    ins = pe.matmul(bank[5][:, P:P + E], ones_bf[:, :], ohs[:, s, :],
                                    start=(s == 0), stop=(s == NT - 1))
                ins.then_inc(cnt_ps, 1)
                pe.wait_ge(ab_ready, l + 1)
                for c in range(8):
                    ins = pe.matmul(bank[6][:, 0:3 * NCOL], aoh[:, c, :], bv[:, c, :],
                                    start=(c == 0), stop=(c == 7))
                ins.then_inc(tb_ps, 1)

            def experts(l):
                pe.wait_ge(tb_ready, l + 1)
                pe.wait_ge(first_right, l + 1)
                iters = pe.value_load(ni[0:1, 1:2], min_val=1, max_val=NBLK // 4)

                def rows_t(q, par, it):
                    pe.wait_ge(xg_in[l][par], 16 * it + 16)
                    pe.wait_ge(xgt_a[l], q + (par + 1))
                    pe.wait_ge(xgt_d[l], q + (par + 1))
                    for k in range(KT):
                        ins = pe.transpose(bank[k // 4][:, (k % 4) * P:(k % 4 + 1) * P],
                                           xg[par][:, k:D:KT], ident[:, :])
                    ins.then_inc(xg_tr[l], 1)

                def gate_up(q, par, it):
                    pe.wait_ge(xgt_a[l], q + (par + 2))
                    pe.wait_ge(xgt_d[l], q + (par + 2))
                    pe.wait_ge(hh_ready[l], q + (par + 1))
                    pe.wait_ge(wgu_in[l][par], 64 * it + 64)
                    for k in range(KT):
                        for b in range(2):
                            ins = pe.matmul(bank[2 + par][B * b:B * (b + 1), :], xgt[par][:, k, B * b:B * (b + 1)],
                                            wgu[:, par, b, :, k, :], start=(k == 0), stop=(k == KT - 1))
                    ins.then_inc(gu_done[l], 1)

                def down(q, par, it):
                    pe.wait_ge(hh_ready[l], q + (par + 3))
                    for k in range(2):
                        ins = pe.transpose(bank[4][:, k * P:(k + 1) * P], hh[par][:, k:F:2], ident[:, :])
                    ins.then_inc(ht_tr[l], 1)
                    pe.wait_ge(ht_sb[l], q + (par + 1))
                    pe.wait_ge(wd_in[l][par], 32 * it + 32)
                    pe.wait_ge(ya_ready[l], q + (par + 1))
                    pe.wait_ge(yd_ready[l], q + (par + 1))
                    for n in range(2):
                        for k in range(2):
                            for b in range(2):
                                ins = pe.matmul(bank[5 + n][B * b:B * (b + 1), :], htt[par][:, k, B * b:B * (b + 1)],
                                                wd[:, par, b, k, n * 512:(n + 1) * 512],
                                                start=(k == 0), stop=(k == 1))
                    ins.then_inc(dn_done[l], 1)

                with pe.Fori(0, iters) as it:
                    q = 2 * it
                    rows_t(q, 0, it)
                    gate_up(q, 0, it)
                    rows_t(q, 1, it)
                    down(q, 0, it)
                    gate_up(q, 1, it)
                    down(q, 1, it)

            router(0)
            experts(0)
            pe.wait_ge(ln_out, 8)
            pe.wait_ge(moe_done[0], 1)
            transpose_tiles(KT, lambda k, t: h[:, t, k * P:(k + 1) * P])
            pe.wait_ge(xt_l, 3 * KT)
            for i in range(2):
                chunk(10 + i, 8 + i, U_ODD + 2 * i, 4 * i)
            with pe.Fori(1, 3) as g:
                for i in range(2):
                    chunk(2 * g + (10 + i), 2 * g + (8 + i), 4 * g + (U_ODD + 2 * i), 4 * i)
            for g in range(3):
                chunk(16 + g, 14 + g, U_ODDV + 2 * g, 4 * (g % 2), by_residue if g else in_order)
            pe.wait_ge(ev_a, 17 + 2)
            pe.wait_ge(ev_d, 19 + 2)

            def pair_tile(hp, g, cols):
                return k3[:, g, ds(hp, 1), cols].rearrange("p a t -> p (a t)")

            def odd_scores(hp, k):
                par, lay, pair = k // 2 % 2, k % 2, hp + k // 4
                pe.wait_ge(qz_ready, 2 * hp + (k // 2 + 1))
                for t in range(NT):
                    blk = slice(t * P, (t + 1) * P)
                    bk = bank[2 * lay + t // 2][:, 256 * (t % 2):256 * (t % 2) + 256]
                    if lay == 0 and t == 0:
                        ins = pe.matmul(bk[:, P:256], qz[par][:, 0, blk], pair_tile(pair, 0, blk),
                                        start=True, stop=True)
                    elif lay == 0:
                        ins = pe.matmul(bk, qz[par][:, 0, blk], pair_tile(pair, 0, slice((t - 1) * P, (t + 1) * P)),
                                        start=True, stop=True)
                    else:
                        for g in (1, 2):
                            ins = pe.matmul(bk[:, (g - 1) * P:g * P], qz[par][:, g, blk],
                                            pair_tile(pair, g, blk), start=True, stop=True)
                ins.then_inc(s2_ready, 1)

            def weights_t(hp, k):
                lay = k % 2
                pe.wait_ge(p_ready, 4 * hp + (k + 1))
                for t in range(NT):
                    for c in range(2):
                        if lay == 0 and t == 0 and c == 0:
                            continue
                        ins = pe.transpose(bank[4 + t // 2][:, 256 * (t % 2) + c * P:256 * (t % 2) + (c + 1) * P],
                                           sc[lay][:, t, c * P:(c + 1) * P], ident[:, :])
                ins.then_inc(t_ready, 1)

            def odd_mix(hp, k):
                par, lay = k // 2, k % 2
                pe.wait_ge(pta, 4 * hp + (k + 1))
                pe.wait_ge(ptd, 4 * hp + (k + 1))
                pe.wait_ge(oe_ready, 4 * hp + (k + 1))
                hv = lambda g, t: v3[:, g, t, ds((2 * hp + par) * DH, DH)]
                for t in range(NT):
                    o = bank[6 + lay][:, t * DH:(t + 1) * DH]
                    w = lambda c: ptt[lay][:, t, c * P:(c + 1) * P]
                    if lay == 0 and t == 0:
                        ins = pe.matmul(o, w(1), hv(0, 0), start=True, stop=True)
                    else:
                        g = (0, 0) if lay == 0 else (1, 2)
                        s = (t - 1, t) if lay == 0 else (t, t)
                        pe.matmul(o, w(0), hv(g[0], s[0]), start=True, stop=False)
                        ins = pe.matmul(o, w(1), hv(g[1], s[1]), start=False, stop=True)
                ins.then_inc(o2_ready, 1)

            def pair_steps(hp, last):
                for k in range(4):
                    weights_t(hp, k)
                    if not (last and k >= 2):
                        odd_scores(hp, k + 2)
                    odd_mix(hp, k)

            odd_scores(0, 0)
            odd_scores(0, 1)
            with pe.Fori(0, 3) as hp:
                pair_steps(hp, False)
            pair_steps(3, True)

            for hp in range(4):
                pe.wait_ge(yo_ready, hp + 1)
                for t in range(NT):
                    ins = pe.transpose(bank[hp][:, t * P:(t + 1) * P], q3[:, 0, hp, t * P:(t + 1) * P], ident[:, :])
                ins.then_inc(xt_ps, 1)
            pe.wait_ge(xt_l, 3 * KT + 4)
            for c in range(2):
                unit(U_WOUT2 + c, c, 0, lambda i: bank[4 * (1 - c) + i][:, :], in_order, nk=4)
            router(1)
            experts(1)


_INS = ["x", "w_in_even", "i_bias", "f_bias", "conv_w", "conv_b", "mlstm_norm_g", "ret_norm_g", "w_out_even",
        "w_in_odd", "w_out_odd", "router_w", "router_bias", "w_gate", "w_up", "w_down", "ln_g", "ln_b"]


def kernel(**inputs):
    import numpy as _np
    import concourse.bacc as _bacc
    from concourse import mybir as _mybir
    from concourse.bass_utils import run_bass_kernel_spmd as _run

    nc = _bacc.Bacc("TRN2", target_bir_lowering=False, num_devices=1)
    arrays, args = {}, []
    for name in _INS:
        a = _np.ascontiguousarray(inputs[name])
        arrays[f"in_{name}"] = a
        args.append(nc.dram_tensor(f"in_{name}", a.shape, _mybir.dt.from_np(a.dtype), kind="ExternalInput").ap())
    o = nc.dram_tensor("out", inputs["x"].shape, _mybir.dt.float32, kind="ExternalOutput").ap()
    trunk(nc, *args, o)
    r = _run(nc, [arrays], core_ids=[0])
    return r.results[0]["out"]
```

```python
import concourse.bass as bass
from concourse import mybir
from contextlib import ExitStack, contextmanager


class Count:

    def __init__(self, eng, name="count"):
        self.eng, self.reg = eng, eng.alloc_register(name)

    def wait(self, sem, value, met):
        self.eng.reg_mov(self.reg, value)
        value = self.eng.snap(self.reg)
        self.eng.wait_ge(met, 1)
        self.eng.wait_ge(sem, value)


class Order:

    def __init__(self, eng, sem, count=None):
        self.eng, self.sem, self.n, self.loop = eng, sem, 0, None
        self.count = count or Count(eng)

    def __call__(self, ins, plain=False):
        self.n += 1
        ins.then_inc(self.sem, 1)
        value = self.n if self.loop is None else self.loop + self.n
        if plain:
            self.count.wait(self.sem, value, self.sem)
        else:
            self.eng.wait_ge(self.sem, value)

    @contextmanager
    def rolled(self, i, per_iter, iters):
        start = self.n
        self.loop, self.n = i * per_iter + start, 0
        yield
        assert self.n == per_iter, f"{self.n} links per iteration, not {per_iter}"
        self.loop, self.n = None, start + per_iter * iters


def trunk(nc, x, w_in_even, i_bias, f_bias, conv_w, conv_b, mlstm_norm_g, ret_norm_g, w_out_even,
          w_in_odd, w_out_odd, router_w, router_bias, w_gate, w_up, w_down, ln_g, ln_b, out):
    f32, f32r, bf16 = mybir.dt.float32, mybir.dt.float32r, mybir.dt.bfloat16
    i32, u32 = mybir.dt.int32, mybir.dt.uint32
    ALU, ACT, AX = mybir.AluOpType, mybir.ActivationFunctionType, mybir.AxisListType
    ds = bass.ds

    P = 128
    T, D = x.shape[1], x.shape[2]
    NT, KT = T // P, D // P
    HD = D // 8
    NH = 4
    VW = HD + 1
    DH = D // 16
    E, EG = w_gate.shape[1], 8
    F = w_gate.shape[3]
    B = 64
    NBLK = 48
    NPAIR = NBLK // 2
    NCOL = NPAIR + 4
    EMPTY = 4096
    ALPHA = 4.0 ** 0.25
    EPS = 1e-5
    BIG = 1e30
    C = 512
    SCALE = HD ** -0.5
    OFF = (0, 512, 896, 1152)
    IN_QR = 4 * NH * HD + 2 * NH
    GATE0 = 4 * NH * HD
    LOG_GAMMA = [-0.03174869831458027, -0.01574835696813892, -0.007843177461025893, -0.003913899321136329]
    SLOPES = [2.0 ** -(h + 1) for h in range(8)]

    ctx = ExitStack()
    with ctx:
        KB = 1024
        BASE = 20 * KB

        class Zone:
            def __init__(self, start, size):
                self.at, self.end = start, start + size

            def take(self, name, shape, dt):
                n = 1
                for s in shape[1:]:
                    n *= s
                n *= 2 if dt == bf16 else 4
                t = nc.alloc_sbuf_tensor_at(name, shape, dt, offset=self.at)
                self.at += (n + 31) // 32 * 32
                assert self.at <= self.end, name
                return t

        const = Zone(BASE, 18 * KB)
        ident = const.take("ident", [P, P], f32)
        dist = const.take("dist", [P, T], f32)
        mask = const.take("mask", [P, P], f32)
        near = const.take("near", [P, 2, 256], f32)
        before = const.take("before", [P, P], bf16)
        ones_bf = const.take("ones_bf", [P, P], bf16)
        rw = const.take("rw", [P, KT, E], f32)
        rb = const.take("rb", [P, E], f32)
        row128 = const.take("row128", [P, P], f32)
        thr = const.take("thr", [P, 8], f32)
        dst_of = const.take("dst_of", [P, 2, NT], f32)
        lgam = const.take("lgam", [P, NH], f32)
        nslope = const.take("nslope", [P, 8], f32)
        cw = const.take("cw", [P, 8, 5], f32)
        gb = const.take("gb", [64, 1], f32)
        sel4 = const.take("sel4", [4, NH, P], f32)
        cwr = Zone(const.at, 4 * KB).take("cwr", [5, D], f32)
        lngb = const.take("lngb", [P, 2, D], f32)
        stat = const.take("stat", [P, 8, 6], f32)
        mv = const.take("mv", [P, 8, 2], f32)
        rstd = const.take("rstd", [P, 8], f32)
        nmr = const.take("nmr", [P, 8], f32)
        nwt = const.take("nwt", [P, 8], f32)
        one = const.take("one", [P, 1], f32)
        warm = const.take("warm", [1, 1], f32)
        h = Zone(BASE + 18 * KB, 16 * KB).take("h", [P, NT, D], f32)

        XZ = BASE + 34 * KB
        z = Zone(XZ, 32 * KB)
        xt_hi = z.take("xt_hi", [P, KT, T], f32r)
        xt_lo = z.take("xt_lo", [P, KT, T], f32r)
        z = Zone(XZ, 32 * KB)
        ks = [z.take(f"ks{i}", [P, T], f32) for i in range(2)]
        pt = [[z.take(f"pt0{i}", [P, 1280], f32) for i in range(2)]]
        dd = [z.take(f"dd{i}", [P, 1280], f32) for i in range(2)]
        mbd = [z.take(f"mbd{i}", [P, NT, P], f32) for i in range(2)]
        hm = [z.take(f"hm{i}", [P, NT, HD], f32) for i in range(2)]
        z = Zone(XZ, 32 * KB)
        qz = [z.take(f"qz{i}", [P, 3, T], f32) for i in range(2)]
        sc = [z.take(f"sc{i}", [P, NT, 256], f32) for i in range(2)]
        ptt = [z.take(f"ptt{i}", [P, NT, 256], f32) for i in range(2)]
        bh = [z.take(f"bh{i}", [P, 2, 256], f32) for i in range(2)]
        z = Zone(XZ, 32 * KB)
        ht = z.take("ht", [P, KT, T], f32)
        z = Zone(XZ, 32 * KB)
        h_lo = z.take("h_lo", [P, NT, D], f32r)
        h_hi = z.take("h_hi", [P, NT, D], f32r)

        R = BASE + 66 * KB
        z = Zone(R, 48 * KB)
        raw = [z.take(f"raw{i}", [P, 4, C], f32) for i in range(2)]
        z2 = Zone(R, 16 * KB)
        pt.append([z2.take(f"pt1{i}", [P, 1280], f32) for i in range(2)])
        wh = [z.take(f"wh{i}", [P, 4, C], f32r) for i in range(2)]
        wl = [z.take(f"wl{i}", [P, 4, C], f32r) for i in range(2)]
        z = Zone(R + 48 * KB, 90 * KB)
        qk = z.take("qk", [P, 2, 2, NH, T], f32)
        v = z.take("v", [P, 2, NT, NH, VW], f32)
        pads = Zone(z.at, 8 * KB)
        wif_hi = pads.take("wif_hi", [P, KT, P], f32r)
        wif_lo = pads.take("wif_lo", [P, KT, P], f32r)
        og = z.take("og", [P, 2, NT, NH * HD], f32)
        mb = z.take("mb", [P, NH, T], f32)
        rows = z.take("rows", [64, T], f32)
        mrow = z.take("mrow", [4, T], f32)
        zf = z.take("zf", [4, T], f32)
        ex = z.take("ex", [4, T], f32)
        gn = z.take("gn", [P, 2, NH * HD], f32)
        cta = z.take("cta", [P, T], f32)
        ctb = z.take("ctb", [P, T], f32)
        jdiff = z.take("jdiff", [P, P], i32)
        z = Zone(R + 48 * KB, 90 * KB)
        q3 = z.take("q3", [P, 3, 4, T], f32)
        k3 = z.take("k3", [P, 3, 4, T], f32)
        v3 = z.take("v3", [P, 3, NT, 8 * DH], f32)
        ms = z.take("ms", [P, 2, NT, 8], f32)
        dn = z.take("dn", [P, 2, NT, 8], f32)
        me = z.take("me", [P, NT, 16], f32)
        mx = z.take("mx", [P, NT, 8], f32)
        w1 = z.take("w1", [P, NT, 8], f32)
        w2 = z.take("w2", [P, NT, 8], f32)
        dsum = z.take("dsum", [P, NT, 8], f32)
        mm = [z.take(f"mm{i}", [P, NT], f32) for i in range(2)]
        nm = [z.take(f"nm{i}", [P, NT], f32) for i in range(2)]
        z = Zone(R, 138 * KB)
        wgu = z.take("wgu", [P, 2, 2, 2, KT, F], f32)
        wd = z.take("wd", [P, 2, 2, 2, D], f32)
        y2z = Zone(z.at - 32 * KB, 32 * KB)
        xgt = z.take("xgt", [P, KT, 2 * P], f32)
        aoh = z.take("aoh", [P, 8, P], f32)
        bv = z.take("bv", [P, 8, 2 * NCOL], f32)
        route_z = Zone(z.at, 6 * KB)
        y2 = [y2z.take(f"y2{i}", [P, 2 * D], f32) for i in range(NT)]
        sel = route_z.take("sel", [P, NT, E], f32)
        msel = route_z.take("msel", [P, NT, E], f32)
        m8g = route_z.take("m8g", [P, NT, 4, 8], f32)
        t1 = route_z.take("t1", [P, 2, NT, E], f32)
        cm = route_z.take("cm", [P, E, 8], f32)
        nb = route_z.take("nb", [P, E], f32)
        bend = route_z.take("bend", [P, E], f32)
        bst = route_z.take("bst", [P, E], f32)
        pos = route_z.take("pos", [P, NT, E], f32)
        sg = [z.take(f"sg{i}", [P, F], f32) for i in range(2)]
        hh = [z.take(f"hh{i}", [P, F], f32) for i in range(2)]
        htt = [z.take(f"htt{i}", [P, 2, P], f32) for i in range(2)]
        cmp = Zone(z.at, 8 * KB).take("cmp", [1, NBLK, E], f32)
        yt = [z.take(f"yt{i}", [P, D], f32) for i in range(2)]
        pick = z.take("pick", [P, NT, 2 * P], f32r)
        pick0 = z.take("pick0", [P, NT, P], f32)
        aff = z.take("aff", [P, NT, E], f32)
        gs = z.take("gs", [P, NT, 8], f32)
        gm = z.take("gm", [P, NT, 8], f32)
        gi = z.take("gi", [P, NT, 8], u32)
        gif = z.take("gif", [P, NT], f32)
        pen = z.take("pen", [P, NT, 4], f32)
        v8 = z.take("v8", [P, NT, 8], f32)
        i8 = z.take("i8", [P, NT, 8], u32)
        ef = z.take("ef", [P, 2, NT], f32)
        oh = z.take("oh", [P, 2, NT, E], f32)
        ohs = z.take("ohs", [P, NT, E], bf16)
        ga = z.take("ga", [P, 2, NT], f32)
        gd = z.take("gd", [P, NT], f32)
        ber = z.take("ber", [1, NBLK], f32)
        be = z.take("be", [1, NBLK], i32)
        ni = z.take("ni", [1, 3], i32)
        dest = z.take("dest", [P, 8], f32)
        di = z.take("di", [P, 8], i32)
        pf = z.take("pf", [P, 8], f32)
        rm = z.take("rm", [P, 8], f32)
        eq = z.take("eq", [P, 8, NCOL], f32)
        td = z.take("td", [P, NCOL], i32)
        gt = z.take("gt", [P, NCOL], f32)
        sidx = [z.take(f"sidx{i}", [P, 1], i32) for i in range(2)]
        z = Zone(20480 - 3 * KB, 3 * KB)
        uc = z.take("uc", [P, NT, 64], f32)
        en = z.take("en", [P, NT, NH], f32)
        wif = z.take("wif", [P, KT, 8], f32)

        bank = [ctx.enter_context(nc.psum_tensor(f"bank{i}", [P, 512], f32)) for i in range(8)]

        y_rows = [nc.dram_tensor(f"y_rows{i}", [2 * T, D], f32).ap() for i in range(2)]
        SR = 8 * DH + 16
        far = nc.dram_tensor("far_rows", [T, SR], f32).ap()

        def sem(name):
            return ctx.enter_context(nc.semaphore(name))

        x_in, gate_in, cw_in, gb_in, gn_in, rw_in = (sem(s) for s in
            ("x_in", "gate_in", "cw_in", "gb_in", "gn_in", "rw_in"))
        ln_in = sem("ln_in")
        consts = sem("consts_ready")
        xt_ps, xt_h, xt_l = sem("xt_in_psum"), sem("xt_hi_ready"), sem("xt_lo_ready")
        raw_in = [sem("raw_in0"), sem("raw_in1")]
        w_hi, w_lo = sem("w_hi_ready"), sem("w_lo_ready")
        unit_done = sem("unit_done")
        ev_a, ev_d = sem("evacuated_act"), sem("evacuated_dve")
        act_o, dve_o, pool_o = sem("act_order"), sem("dve_order"), sem("pool_order")
        gate_zero, gate_hi, gate_lo, gate_tr = (sem(s) for s in
            ("gate_w_zeroed", "gate_w_hi", "gate_w_lo", "gate_rows_in_psum"))
        gate_exp, gate_ln, rows_ready = sem("gate_neg_abs"), sem("gate_softplus"), sem("rows_ready")
        cw_ps, cw_sb = sem("conv_taps_in_psum"), sem("conv_taps_ready")
        conv_done, silu_done = sem("conv_done"), sem("qk_silu_done")
        og_act, og_ready = sem("output_gates_act"), sem("output_gates_ready")
        mb_ps, mb_sb, uc_ps, uc_sb, en_sb = (sem(s) for s in
            ("m_rows_in_psum", "m_rows_ready", "u_cols_in_psum", "u_cols_ready", "exp_neg_m_ready"))
        ks_ready, s_ready, d_ready, pt_ready, o_ready = (sem(s) for s in
            ("k_staged", "scores_ready", "decay_ready", "weights_ready", "heads_out_ready"))
        mbd_ready, o_read, yn_ready, y_done = (sem(s) for s in
            ("masked_m_ready", "heads_out_read", "head_normed", "y_done"))
        ln_nmr, ln_norm, ln_scaled = (sem(s) for s in ("ln_coeffs", "ln_normed", "ln_scaled"))
        ln_out = [sem("ln_out_even_tiles"), sem("ln_out_odd_tiles")]
        hi_ready, lo_ready = sem("h_hi_ready"), sem("h_lo_ready")
        pick_ready, pick_o = ([sem(f"{s}{l}") for l in range(2)] for s in ("pick_ready", "pick_order"))
        rt_ps, rt_sb, lg_ps, aff_ready = (sem(s) for s in
            ("router_xt_in_psum", "router_xt_ready", "logits_in_psum", "affinities_ready"))
        oh_ready, cnt_ps, blk_ready, ab_ready, tb_ps, tb_ready = (sem(s) for s in
            ("onehots_ready", "counts_in_psum", "blocks_ready", "table_terms_ready",
             "tables_in_psum", "tables_ready"))
        wgu_in = [[sem(f"gate_up_in{l}{i}") for i in range(2)] for l in range(2)]
        wd_in = [[sem(f"down_in{l}{i}") for i in range(2)] for l in range(2)]
        y_out = [[sem(f"rows_scattered{l}{i}") for i in range(2)] for l in range(2)]
        (xg_tr, xgt_a, xgt_d, gu_done, sg_ready, hh_ready, ht_tr, ht_sb, dn_done, ya_ready,
         yd_ready, idx_ready, moe_done) = (
            [sem(f"{s}{l}") for l in range(2)] for s in
            ("rows_picked", "xgt_ready_act", "xgt_ready_dve", "gate_up_done", "silu_ready",
             "hidden_ready", "hidden_transposed", "hidden_t_ready", "down_done", "y_ready_act",
             "y_ready_dve", "pool_indices", "moe_done"))
        y2_in = [sem(f"y2_in{t}") for t in range(NT)]
        bh_ready, qz_ready = sem("bias_ready"), sem("q_staged")
        s2_ready, sb_ready, nm_ready, p_ready = (sem(s) for s in
            ("odd_scores", "odd_biased", "odd_neg_max", "odd_weights"))
        t_ready, pta, ptd, o2_ready, oe_ready = (sem(s) for s in
            ("odd_weights_t", "odd_wt_act", "odd_wt_dve", "odd_out", "odd_out_kept"))
        far_out, far_in = sem("far_rows_stored"), sem("far_rows_loaded")
        mx_ready, we_ready, wn_ready, far_scaled, yo_ready = (sem(s) for s in
            ("merge_max", "merge_exp", "merge_weights", "far_scaled", "odd_y_ready"))
        out_stored = sem("out_stored")
        first_right, reloaded = sem("first_weights_right"), [sem(f"first_weights_reloaded{l}") for l in range(2)]

        xe, xo = w_in_even[0], w_in_odd[0]
        woe, woo = w_out_even[0], w_out_odd[0]
        U_WOUT, U_ODD, U_ODDV, U_WOUT2 = 16, 20, 32, 38

        def unit_src(w, row0, col):
            return w[row0:row0 + 4 * P, col].rearrange("(k p) c -> p k c", p=P)

        def perm(ap):
            return ap.rearrange("p (j a) -> p a j", a=4)

        def wait_ln(eng, n, t):
            eng.wait_ge(ln_out[t % 2], 2 * n + t // 2 + 1)

        def mlstm_out(par, t):
            return bank[6 + par][:, t * VW:(t + 1) * VW] if t < 3 else bank[3 * par + 2][:, 256:256 + VW]

        block = ctx.enter_context(nc.Block())

        @block.sync
        def _(sp):
            sp.dma_start(h[:, :, :], x[0].rearrange("(t p) d -> p t d", p=P)).then_inc(x_in, 16)

            def load_unit(u, slot, w, row0, col):
                sp.wait_ge(w_lo, u + 1)
                sp.dma_start(raw[slot][:, :, :], unit_src(w, row0, col)).then_inc(raw_in[slot], 16)

            def load_ln(n):
                for t in (2, 3) if n else ():
                    wait_ln(sp, n - 1, t)
                for i, w in enumerate((ln_g, ln_b)):
                    sp.dma_start(lngb[:, i, :], w[n // 2, n % 2:n % 2 + 1, :].to_broadcast([P, D]))\
                      .then_inc(ln_in, 16)

            def load_gate_up(l, par, experts, done):
                for b, e in enumerate(experts):
                    for i, w in enumerate((w_gate, w_up)):
                        sp.dma_start(wgu[:, par, b, i, :, :].rearrange("p k f -> p (k f)"),
                                     w[l][ds(e, 1)].rearrange("a (p k) f -> p (a k f)", p=P)).then_inc(done, 16)

            def load_down(l, par, experts, done):
                for b, e in enumerate(experts):
                    sp.dma_start(wd[:, par, b, :, :].rearrange("p k n -> p (k n)"),
                                 w_down[l][ds(e, 1)].rearrange("a (p k) n -> p (a k n)", p=P)).then_inc(done, 16)

            def early_down(l):
                for par in range(2):
                    load_down(l, par, (2 * par, 2 * par + 1), wd_in[l][par])

            def early_gate_up(l):
                for par in range(2):
                    load_gate_up(l, par, (2 * par, 2 * par + 1), wgu_in[l][par])

            def expert_weights(l):
                sp.wait_ge(blk_ready, l + 1)
                iters = sp.value_load(ni[0:1, 1:2], min_val=1, max_val=NBLK // 4)
                wrong = sp.value_load(ni[0:1, 2:3], min_val=0, max_val=1)

                def block_experts(j):
                    return [sp.value_load(be[0:1, ds(j + b, 1)], min_val=0, max_val=E - 1) for b in range(2)]

                with sp.If(wrong > 0):
                    for par in range(2):
                        sp.wait_ge(wgu_in[l][par], 64)
                        sp.wait_ge(wd_in[l][par], 32)
                    for par in range(2):
                        e = block_experts(2 * par)
                        load_gate_up(l, par, e, reloaded[l])
                        load_down(l, par, e, reloaded[l])
                    sp.wait_ge(reloaded[l], 12 * 16)
                sp.sem_inc(first_right, 1)
                with sp.Fori(1, iters) as it:
                    e = [block_experts(4 * it + 2 * par) for par in range(2)]
                    for par in range(2):
                        sp.wait_ge(gu_done[l], 2 * it + par + 1)
                        load_gate_up(l, par, e[par], wgu_in[l][par])
                    for par in range(2):
                        sp.wait_ge(dn_done[l], 2 * it + par + 1)
                        load_down(l, par, e[par], wd_in[l][par])

            def load_y(l):
                sp.wait_ge(moe_done[l], 1)
                for t in range(NT):
                    sp.dma_start(y2[t][:, :], y_rows[l][2 * t * P:2 * (t + 1) * P, :]
                                 .rearrange("(p c) d -> p (c d)", c=2)).then_inc(y2_in[t], 16)

            with sp.Fori(0, 2) as j:
                for i in range(4):
                    for half in range(2):
                        load_unit(8 * j + 2 * i + half, half, xe, half * 4 * P, ds(j * IN_QR + i * C, C))
            load_ln(0)
            for c in range(2):
                if c:
                    sp.wait_ge(o_ready, 8)
                for half in range(2):
                    load_unit(U_WOUT + 2 * c + half, half, woe, half * 4 * P, slice(c * C, (c + 1) * C))
            early_down(0)
            sp.wait_ge(unit_done, U_ODD + 2)
            early_gate_up(0)
            load_ln(1)
            expert_weights(0)
            load_y(0)
            with sp.Fori(0, 3) as g:
                for i in range(2):
                    for half in range(2):
                        load_unit(4 * g + (U_ODD + 2 * i + half), half, xo, half * 4 * P,
                                  ds(g * (3 * C) + i * C, C))
            for g in range(3):
                for half in range(2):
                    load_unit(U_ODDV + 2 * g + half, half, xo, half * 4 * P,
                              slice(3 * C * g + 2 * C, 3 * C * (g + 1)))
            for c in range(2):
                load_unit(U_WOUT2 + c, c, woo, 0, slice(c * C, (c + 1) * C))
            load_ln(2)
            farv = far.rearrange("(j a) c -> j a c", a=4)
            for hp in range(4):
                sp.wait_ge(oe_ready, 4 * hp + 4 + 2)
                sp.dma_start(farv[:, :, 2 * DH * hp:2 * DH * (hp + 1)],
                             q3[:, 1, hp, :].rearrange("p (a c) -> p a c", a=NT)).then_inc(far_out, 16)
            sp.dma_start(farv[:, :, 8 * DH:8 * DH + 8], ms[:, 1, :, :]).then_inc(far_out, 16)
            sp.dma_start(farv[:, :, 8 * DH + 8:], dn[:, 1, :, :]).then_inc(far_out, 16)
            sp.wait_ge(far_out, 6 * 16)
            fart = far.rearrange("(t p) c -> p t c", p=P)
            sp.dma_start(me[:, :, :], fart[:, :, 8 * DH:]).then_inc(far_in, 16)
            sp.dma_start(q3[:, 2, :, :], fart[:, :, 0:8 * DH]).then_inc(far_in, 16)
            sp.wait_ge(yo_ready, 4)
            early_down(1)
            sp.wait_ge(unit_done, U_WOUT2 + 2 + 2)
            early_gate_up(1)
            load_ln(3)
            expert_weights(1)
            load_y(1)
            for t in range(NT):
                wait_ln(sp, 3, t)
                sp.dma_start(out[0, t * P:(t + 1) * P, :], h[:, t, :]).then_inc(out_stored, 16)
            sp.wait_ge(out_stored, 16 * NT)

        @block.gpsimd
        def _(pool):
            link = Order(pool, pool_o)
            column_reg = pool.alloc_register("column")

            def column(value):
                pool.reg_mov(column_reg, value)
                return pool.snap(column_reg, min_val=0, max_val=NCOL - 1)

            pool.memset(wif_hi[:, :, :].bitcast(f32), 0.0)
            pool.memset(wif_lo[:, :, :].bitcast(f32), 0.0).then_inc(gate_zero, 1)
            for t in (ident, mask):
                pool.memset(t[:, :], 0.0)
            pool.memset(before[:, :], 1.0)
            pool.memset(ones_bf[:, :], 1.0)
            pool.memset(one[:, :], 1.0)
            pool.memset(rows[:, :], 0.0)
            pool.memset(sel4[:, :, :], 0.0)
            pool.memset(near[:, :, :], BIG)
            pool.memset(v[:, 0, :, :, HD:VW], 1.0)
            pool.memset(v[:, 1, :, :, HD:VW], 1.0)
            for i in range(NH):
                pool.memset(lgam[:, i:i + 1], LOG_GAMMA[i])
            for i in range(8):
                pool.memset(nslope[:, i:i + 1], -SLOPES[i])
                pool.memset(thr[:, i:i + 1], float(B * i))
            exact = dict(allow_small_or_imprecise_dtypes=True)
            pool.iota(dist[:, :], pattern=[[1, T]], base=0, channel_multiplier=-1, **exact)
            pool.iota(row128[:, :], pattern=[[1, P]], base=0, channel_multiplier=0, **exact)
            link(pool.iota(dst_of[:, :, :], pattern=[[1, 2], [2 * P, NT]], base=-EMPTY,
                           channel_multiplier=2, **exact))
            pool.affine_select(out=ident[:, :], in_=ident[:, :], compare_op=ALU.not_equal, fill=1.0,
                               base=0, pattern=[[-1, P]], channel_multiplier=1)
            pool.affine_select(out=mask[:, :], in_=mask[:, :], compare_op=ALU.is_ge, fill=BIG,
                               base=0, pattern=[[1, P]], channel_multiplier=-1)
            pool.affine_select(out=before[:, :], in_=before[:, :], compare_op=ALU.is_gt, fill=0.0,
                               base=0, pattern=[[1, P]], channel_multiplier=-1)
            pool.affine_select(out=sel4[:, :, :], in_=sel4[:, :, :], compare_op=ALU.not_equal, fill=1.0,
                               base=0, pattern=[[-1, NH], [0, P]], channel_multiplier=1)
            pool.affine_select(out=dist[:, :], in_=dist[:, :], compare_op=ALU.is_ge, fill=BIG,
                               base=0, pattern=[[1, T]], channel_multiplier=-1)
            link(pool.iota(near[:, 0, :], pattern=[[-1, 256]], base=P, channel_multiplier=1, **exact))
            link(pool.affine_select(out=near[:, 0, :], in_=near[:, 0, :], compare_op=ALU.is_ge, fill=BIG,
                                    base=P, pattern=[[-1, 256]], channel_multiplier=1))
            link(pool.affine_select(out=near[:, 0, :], in_=near[:, 0, :], compare_op=ALU.is_ge, fill=BIG,
                                    base=0, pattern=[[1, 256]], channel_multiplier=-1))
            for c in (0, P):
                pool.iota(near[:, 1, c:c + P], pattern=[[-4, P]], base=0, channel_multiplier=4, **exact)
            link(pool.iota(jdiff[:, :], pattern=[[-1, P]], base=P, channel_multiplier=1))
            for c in (0, P):
                last = pool.affine_select(out=near[:, 1, c:c + P], in_=near[:, 1, c:c + P],
                                          compare_op=ALU.is_ge, fill=BIG, base=0, pattern=[[-4, P]],
                                          channel_multiplier=4)
            last.then_inc(consts, 1)

            pool.wait_ge(cw_sb, 1)
            pool.wait_ge(ev_a, 2 + 2)
            pool.wait_ge(ev_d, 2 + 2)
            qk_m = qk[:, 0, :, :, :].rearrange("p a h t -> p (a h) t")
            pool.wait_ge(consts, 1)
            with pool.Fori(0, 8) as i, link.rolled(i, 9, 8):
                xi = qk_m[:, ds(i, 1), :].rearrange("p a t -> p (a t)")

                def tap(m, n):
                    return cw[:, ds(i, 1), m:m + 1].rearrange("p a b -> p (a b)").to_broadcast([P, n])

                link(pool.tensor_tensor(cta[:, :], xi, tap(3, T), ALU.mult))
                link(pool.tensor_tensor(cta[:, :], cta[:, :], tap(4, T), ALU.add))
                for s in (1, 2, 3):
                    link(pool.tensor_tensor(ctb[:, s:T], xi[:, 0:T - s], tap(3 - s, T - s), ALU.mult))
                    link(pool.tensor_tensor(cta[:, s:T], cta[:, s:T], ctb[:, s:T], ALU.add), plain=(s == 3))
                link(pool.tensor_copy(xi, cta[:, :]))
            pool.tensor_copy(ctb[:, 0:1], cta[:, 0:1]).then_inc(conv_done, 1)

            pool.wait_ge(og_act, 1)
            pool.wait_ge(gn_in, 32)
            pool.tensor_tensor(og[:, 1, :, :], og[:, 1, :, :],
                               gn[:, 1:2, :].to_broadcast([P, NT, NH * HD]), ALU.mult).then_inc(og_ready, 1)
            pool.wait_ge(og_ready, 1)

            def masked_m(pair):
                for par in range(2):
                    n = 2 * pair + par
                    if pair == 3:
                        pool.wait_ge(d_ready, n - 1)
                    pool.tensor_tensor(
                        mbd[par][:, :, :], mb[:, n - NH, :].rearrange("p (j t) -> p j t", t=P),
                        mask[:, None, :].to_broadcast([P, NT, P]), ALU.add).then_inc(mbd_ready, 1)

            def head_gain(pair):
                for par in range(2):
                    n = 2 * pair + par
                    pool.wait_ge(yn_ready, n + 1)
                    hd, branch = n % NH, 1 - n // NH
                    dst = og[:, branch, :, hd * HD:(hd + 1) * HD]
                    other = dst if branch else gn[:, 0:1, hd * HD:(hd + 1) * HD].to_broadcast([P, NT, HD])
                    pool.tensor_tensor(dst, hm[par][:, :, :], other, ALU.mult).then_inc(y_done, 1)

            pool.wait_ge(mb_sb, 2)
            masked_m(2)
            head_gain(0)
            masked_m(3)
            head_gain(1)
            head_gain(2)
            head_gain(3)

            def ln_shift(n):
                pool.wait_ge(ln_in, 32 * (n + 1))
                for t in (0, 2):
                    pool.wait_ge(ln_scaled, 2 * n + t // 2 + 1)
                    pool.tensor_tensor(h[:, t, :], h[:, t, :], lngb[:, 1, :], ALU.add).then_inc(ln_out[0], 1)

            def dispatch(l):
                def scatter(par, rows_of):
                    pool.indirect_dma_start(
                        out=y_rows[l], out_offset=bass.IndirectOffsetOnAxis(ap=sidx[par][:, 0:1], axis=0),
                        in_=rows_of, in_offset=None,
                        bounds_check=2 * T - 1, oob_is_err=False).then_inc(y_out[l][par], 16)

                for par in range(2):
                    link(pool.memset(sidx[par][:, :], EMPTY))
                    wait_ln(pool, 2 * l, 2)
                    scatter(par, h[:, 2 * par, :])
                pool.wait_ge(lg_ps, l + 1)
                for t in range(NT):
                    pool.wait_ge(hi_ready, NT * l + t + 1)
                    pool.tensor_tensor(h_lo[:, t, :], h[:, t, :], h_hi[:, t, :], ALU.subtract).then_inc(lo_ready, 1)
                pool.wait_ge(tb_ready, l + 1)
                for par in range(2):
                    pool.wait_ge(y_out[l][par], 16)
                moved = Order(pool, idx_ready[l], link.count)
                iters = pool.value_load(ni[0:1, 1:2], min_val=1, max_val=NBLK // 4)
                with pool.Fori(0, iters) as it, moved.rolled(it, 2, 0):
                    for par in range(2):
                        col = column(2 * it + par)
                        pool.wait_ge(ya_ready[l], 2 * it + (par + 2))
                        pool.wait_ge(yd_ready[l], 2 * it + (par + 2))
                        link.count.wait(y_out[l][par], 16 * it + 16, consts)
                        moved(pool.tensor_copy(sidx[par][:, :], td[:, ds(col, 1)]), plain=True)
                        scatter(par, yt[par][:, :])
                for par in range(2):
                    link.count.wait(y_out[l][par], 16 * iters + 16, consts)
                pool.memset(sidx[0][:, :], 0).then_inc(moe_done[l], 1)

            ln_shift(0)
            dispatch(0)
            ln_shift(1)
            pool.wait_ge(ev_d, 19 + 2)
            pool.wait_ge(ev_a, 17 + 2)
            pool.wait_ge(qz_ready, 1)

            def stage_q(hp, par, first=False):
                rr = slice(64 * par, 64 * par + 64)
                ins = None if first else pool.tensor_copy(qz[par][rr, :, :], q3[rr, :, ds(hp, 1), :].rearrange("p g a t -> p (g a) t"))
                if not first:
                    ins.then_inc(qz_ready, 1)
                if isinstance(hp, int):
                    pool.wait_ge(qz_ready, 2 * hp + par + 1)
                else:
                    link.count.wait(qz_ready, 2 * hp + (par + 1), consts)
                pool.tensor_tensor(bh[par][:, :, :], near[:, :, :],
                                   nslope[:, None, ds(2 * hp + par, 1)].to_broadcast([P, 2, 256]), ALU.mult)\
                    .then_inc(bh_ready, 1)

            stage_q(0, 0, first=True)
            pool.wait_ge(bh_ready, 1)
            stage_q(0, 1)
            with pool.Fori(1, 4) as hp:
                for par in range(2):
                    pool.wait_ge(sb_ready, 4 * hp + (2 * par - 2))
                    pool.wait_ge(bh_ready, 2 * hp + par)
                    link.count.wait(s2_ready, 4 * hp + 2 * par, consts)
                    stage_q(hp, par)
            pool.wait_ge(wn_ready, 1)
            for hp in range(4):
                o2 = q3[:, 2, :, 2 * DH * hp:2 * DH * (hp + 1)].rearrange("p t (u c) -> p t u c", u=2)
                wb = w2[:, :, 2 * hp:2 * hp + 2, None].to_broadcast([P, NT, 2, DH])
                pool.tensor_tensor(o2, o2, wb, ALU.mult).then_inc(far_scaled, 1)
            ln_shift(2)
            dispatch(1)
            ln_shift(3)

        @block.scalar
        def _(act):
            link = Order(act, act_o)
            act.sem_inc(ev_a, 2)
            for l in range(2):
                act.sem_inc(ya_ready[l], 1)
            gates = xe[:, GATE0:GATE0 + 8].rearrange("(k p) c -> p k c", p=P)
            act.dma_start(wif[:, :, :], gates).then_inc(gate_in, 16)
            act.dma_start(cwr[0:4, :], conv_w[0]).then_inc(cw_in, 16)
            act.dma_start(cwr[4:5, :], conv_b).then_inc(cw_in, 16)
            act.dma_start(gb[0:4, :], i_bias.rearrange("a h -> h a")).then_inc(gb_in, 16)
            act.dma_start(gb[32:36, :], f_bias.rearrange("a h -> h a")).then_inc(gb_in, 16)
            act.dma_start(gn[:, 0, :], mlstm_norm_g.to_broadcast([P, NH * HD])).then_inc(gn_in, 16)
            act.dma_start(gn[:, 1, :], ret_norm_g.to_broadcast([P, NH * HD])).then_inc(gn_in, 16)
            act.dma_start(rw[:, :, :], router_w.rearrange("(k p) e -> p k e", p=P)).then_inc(rw_in, 16)
            act.dma_start(rb[:, :], router_bias.rearrange("(a e) -> a e", a=1).to_broadcast([P, E]))\
               .then_inc(rw_in, 16)

            def split_xt(base, tiles):
                for k in tiles:
                    act.wait_ge(xt_ps, base + k + 1)
                    act.activation(xt_hi[:, k, :], bank[k][:, :], ACT.Copy).then_inc(xt_h, 1)

            def split_unit(u, slot):
                act.wait_ge(raw_in[slot], u * 8 + (16 - 8 * slot) if not isinstance(u, int)
                            else 16 * (u // 2 + 1))
                act.wait_ge(unit_done, u + 1)
                act.activation(wh[slot][:, :, :], raw[slot][:, :, :], ACT.Copy).then_inc(w_hi, 1)

            def evacuate(c, dsts, scale=1.0):
                act.wait_ge(unit_done, 2 * c + 4)
                for dst, src in dsts:
                    ins = act.activation(dst, src, ACT.Copy, scale=scale)
                ins.then_inc(ev_a, 1)

            act.wait_ge(gate_in, 16)
            act.wait_ge(gate_zero, 1)
            act.activation(wif_hi[:, :, 0:4], wif[:, :, 0:4], ACT.Copy)
            act.activation(wif_hi[:, :, 32:36], wif[:, :, 4:8], ACT.Copy).then_inc(gate_hi, 1)
            split_xt(0, range(KT))
            for u in range(2):
                split_unit(u, u)
            act.wait_ge(gate_exp, 1)
            link(act.activation(ex[:, :], zf[:, :], ACT.Exp))
            act.activation(ex[:, :], ex[:, :], ACT.Ln, bias=one[0:4, 0:1]).then_inc(gate_ln, 1)
            with act.Fori(0, 2) as j:
                for i in range(4):
                    st = 4 * (i % 2)
                    split_unit(8 * j + (2 * i + 2), 0)
                    if i < 2:
                        dsts = [(qk[:, ds(j, 1), i, b, :].rearrange("p a t -> p (a t)"), bank[st + b][:, :])
                                for b in range(2)]
                    elif i == 2:
                        dsts = [(v[:, ds(j, 1), b, :, 0:HD].rearrange("p a h e -> p (a h) e"),
                                 bank[st + b][:, :].rearrange("p (h e) -> p h e", e=HD)) for b in range(2)]
                    else:
                        dsts = [(og[:, ds(j, 1), b, :].rearrange("p a t -> p (a t)"), bank[st + b][:, :])
                                for b in range(2)]
                    evacuate(4 * j + i, dsts)
                    split_unit(8 * j + (2 * i + 3), 1)
            act.wait_ge(mb_ps, 1)
            for i in range(2):
                ins = act.activation(mb[:, i, :], bank[i][:, :], ACT.Copy)
            ins.then_inc(mb_sb, 1)
            act.wait_ge(consts, 1)
            act.wait_ge(unit_done, 16 + 2)
            act.wait_ge(ev_d, 8 + 2)
            act.wait_ge(ev_a, 8 + 2)

            def stage_k(pair):
                for par in range(2):
                    n = 2 * pair + par
                    if pair:
                        act.wait_ge(s_ready, n - 1)
                    act.activation(ks[par][:, :], qk[:, 1 - n // NH, 1, n % NH, :], ACT.Copy, scale=SCALE)\
                       .then_inc(ks_ready, 1)

            def decays(pair):
                for par in range(2):
                    n = 2 * pair + par
                    if pair:
                        act.wait_ge(pt_ready, n - 1)
                    if n < NH:
                        act.activation(dd[par][:, 0:T], dist[:, :], ACT.Exp, scale=lgam[:, n:n + 1])\
                           .then_inc(d_ready, 1)
                        continue
                    hd = n - NH
                    act.wait_ge(mbd_ready, hd + 1)
                    for kb in range(NT):
                        u_s, left = uc[:, kb, hd:hd + 1], T - P * (kb + 1)
                        if left:
                            act.activation(dd[par][:, OFF[kb] + P:OFF[kb] + P + left], mb[:, hd, P * (kb + 1):T],
                                           ACT.Exp, scale=-1.0, bias=u_s)
                        ins = act.activation(dd[par][:, OFF[kb]:OFF[kb] + P], mbd[par][:, kb, :],
                                             ACT.Exp, scale=-1.0, bias=u_s)
                    ins.then_inc(d_ready, 1)

            stage_k(0)
            decays(0)
            stage_k(1)
            decays(1)
            act.activation(og[:, 1, :, :], og[:, 1, :, :], ACT.Silu).then_inc(og_act, 1)
            act.wait_ge(conv_done, 1)
            act.activation(qk[:, 0, :, :, :], qk[:, 0, :, :, :], ACT.Silu).then_inc(silu_done, 1)
            act.activation(og[:, 0, :, :], og[:, 0, :, :], ACT.Sigmoid)
            act.wait_ge(uc_sb, 1)
            act.activation(en[:, :, :], uc[:, :, 32:32 + NH], ACT.Exp).then_inc(en_sb, 1)
            act.wait_ge(silu_done, 1)
            for pair in (2, 3):
                stage_k(pair)
                decays(pair)
            split_xt(8, range(KT))
            split_unit(U_WOUT + 2, 0)
            split_unit(U_WOUT + 3, 1)

            def ln_normalise(n):
                act.wait_ge(ln_nmr, n + 1)
                for t in range(NT):
                    act.activation(h[:, t, :], h[:, t, :], ACT.Identity, scale=rstd[:, t:t + 1],
                                   bias=nmr[:, t:t + 1]).then_inc(ln_norm, 1)

            def router(l):
                act.activation(warm[:, :], one[0:1, 0:1], ACT.Sigmoid)
                for t in range(NT):
                    act.wait_ge(rt_ps, NT * l + t + 1)
                    for b in range(2):
                        ins = act.activation(ht[:, 4 * b:4 * b + 4, t * P:(t + 1) * P],
                                             bank[2 * (t % 2) + b][:, :].rearrange("p (k t) -> p k t", t=P),
                                             ACT.Copy)
                    ins.then_inc(rt_sb, 1)
                act.wait_ge(lg_ps, l + 1)
                act.activation(aff[:, :, :], bank[4][:, 0:NT * E].rearrange("p (t e) -> p t e", e=E),
                               ACT.Sigmoid).then_inc(aff_ready, 1)
                for t in range(NT):
                    act.activation(h_hi[:, t, :], h[:, t, :], ACT.Copy).then_inc(hi_ready, 1)

            def experts(l):

                def keep_rows(n, half):
                    act.wait_ge(xg_tr[l], 2 * n + (half + 1))
                    act.activation(xgt[:, 4 * half:4 * half + 2, :], bank[0][:, :].rearrange("p (k t) -> p k t", k=2),
                                   ACT.Copy).then_inc(xgt_a[l], 1)

                def silu(q, par):
                    act.wait_ge(gu_done[l], q + (par + 3))
                    act.wait_ge(hh_ready[l], q + (par + 1))
                    act.activation(sg[par][:, :], bank[2 + par][:, 0:F], ACT.Silu).then_inc(sg_ready[l], 1)

                def hidden_t(q, par):
                    act.wait_ge(ht_tr[l], q + (par + 3))
                    act.wait_ge(dn_done[l], q + (par + 1))
                    act.activation(htt[par][:, :, :], bank[4][:, 0:2 * P].rearrange("p (k t) -> p k t", t=P),
                                   ACT.Copy).then_inc(ht_sb[l], 1)

                def y_gated(q, par, it):
                    act.wait_ge(dn_done[l], q + (par + 3))
                    act.wait_ge(y_out[l][par], 16 * it + 16)
                    act.activation(yt[par][:, 0:512], bank[5][:, :], ACT.Copy,
                                   scale=gt[:, ds(q + par, 1)]).then_inc(ya_ready[l], 1)

                for half in range(2):
                    keep_rows(0, half)
                act.wait_ge(tb_ready, l + 1)
                iters = act.value_load(ni[0:1, 1:2], min_val=1, max_val=NBLK // 4)
                with act.Fori(0, iters) as it:
                    q = 2 * it
                    silu(q, 0)
                    silu(q, 1)
                    for par in range(2):
                        keep_rows(it + 1, par)
                        hidden_t(q, par)
                        y_gated(q, par, it)

            ln_normalise(0)
            router(0)
            experts(0)
            ln_normalise(1)

            for u in range(2):
                split_xt(16, range(4 * u, 4 * u + 4))
                split_unit(U_ODD + u, u)

            def odd_evac(c, st, dst, src_of, scale=1.0):
                evacuate(c, [(dst(b), src_of(bank[st + b][:, :])) for b in range(2)], scale)

            def q_scale(i):
                return 1.0 if i else DH ** -0.5

            for i, t in enumerate((q3, k3)):
                split_unit(U_ODD + 2 * i + 2, 0)
                odd_evac(10 + i, 4 * i, lambda b: t[:, 0, b, :], lambda s: s, q_scale(i))
                split_unit(U_ODD + 2 * i + 3, 1)
            with act.Fori(1, 3) as g:
                for i, t in enumerate((q3, k3)):
                    split_unit(4 * g + (U_ODD + 2 * i + 2), 0)
                    odd_evac(2 * g + (10 + i), 4 * i,
                             lambda b: t[:, ds(g, 1), b, :].rearrange("p g (a j) -> p (g a) j", a=4),
                             perm, q_scale(i))
                    split_unit(4 * g + (U_ODD + 2 * i + 3), 1)
            for g in range(3):
                split_unit(U_ODDV + 2 * g + 2, 0)
                odd_evac(16 + g, 4 * (g % 2), lambda b: v3[:, g, b, :], lambda s: s)
                split_unit(U_ODDV + 2 * g + 3, 1)

            def exps(hp, k):
                lay = k % 2
                act.wait_ge(nm_ready, 4 * hp + (k + 1))
                for t in range(NT):
                    cols = slice(P, 256) if (lay == 0 and t == 0) else slice(0, 256)
                    ins = act.activation(sc[lay][:, t, cols], sc[lay][:, t, cols], ACT.Exp,
                                         bias=nm[lay][:, t:t + 1],
                                         accum_out=dn[:, lay, t, ds(2 * hp + k // 2, 1)])
                ins.then_inc(p_ready, 1)

            def keep_weights(hp, k):
                lay = k % 2
                act.wait_ge(t_ready, 4 * hp + (k + 1))
                act.wait_ge(o2_ready, 4 * hp + (k + 1))
                lo = P if lay == 0 else 0
                act.activation(ptt[lay][:, 0:2, :].rearrange("p a c -> p (a c)")[:, lo:512],
                               bank[4][:, lo:512], ACT.Copy).then_inc(pta, 1)

            def pair_steps(hp, last):
                for k in range(4):
                    if not (last and k == 3):
                        exps(hp, k + 1)
                    keep_weights(hp, k)

            exps(0, 0)
            with act.Fori(0, 3) as hp:
                pair_steps(hp, False)
            pair_steps(3, True)
            act.wait_ge(mx_ready, 1)
            link(act.activation(w1[:, :, :], w1[:, :, :], ACT.Exp))
            act.activation(w2[:, :, :], w2[:, :, :], ACT.Exp).then_inc(we_ready, 1)
            split_xt(24, range(4))
            ln_normalise(2)
            router(1)
            experts(1)
            ln_normalise(3)

        @block.vector
        def _(dve):
            link = Order(dve, dve_o)
            dve.sem_inc(w_lo, 2)
            dve.sem_inc(ev_d, 2)
            dve.sem_inc(oe_ready, 2)
            for l in range(2):
                dve.sem_inc(yd_ready[l], 1)
                dve.sem_inc(hh_ready[l], 2)

            def split_xt(base, tiles):
                for k in tiles:
                    dve.wait_ge(xt_h, base + k + 1)
                    dve.tensor_tensor(xt_lo[:, k, :], bank[k][:, :], xt_hi[:, k, :], ALU.subtract)\
                       .then_inc(xt_l, 1)

            def split_unit(u, slot):
                dve.wait_ge(w_hi, u + 1)
                dve.tensor_tensor(wl[slot][:, :, :], raw[slot][:, :, :], wh[slot][:, :, :], ALU.subtract)\
                   .then_inc(w_lo, 1)

            def evacuate(c, dsts, scale=None):
                dve.wait_ge(unit_done, 2 * c + 4)
                for dst, src in dsts:
                    ins = (dve.tensor_scalar(dst, src, scale, None, ALU.mult) if scale
                           else dve.tensor_copy(dst, src))
                ins.then_inc(ev_d, 1)

            def rsqrt(var, n):
                y, w, s = rstd[:, 0:n], nwt[:, 0:n], nmr[:, 0:n]
                link(dve.tensor_scalar(s, var, EPS, None, ALU.add))
                link(dve.tensor_scalar(y.bitcast(i32), s.bitcast(i32), -0.5, 1597463007.0, ALU.mult, ALU.add))
                for _ in range(3):
                    link(dve.scalar_tensor_tensor(w, y, -0.5, y, ALU.mult, ALU.mult))
                    link(dve.tensor_tensor(w, w, s, ALU.mult))
                    link(dve.scalar_tensor_tensor(y, w, 1.5, y, ALU.add, ALU.mult))

            dve.wait_ge(consts, 1)
            quarter, rest = hm[1][:, 0, :], hm[1][:, 1, :]
            link(dve.tensor_scalar(quarter.bitcast(i32), jdiff[:, :], 2, None, ALU.arith_shift_right))
            link(dve.tensor_copy(rest, quarter.bitcast(i32)))
            link(dve.tensor_copy(quarter, jdiff[:, :]))
            link(dve.scalar_tensor_tensor(rest, rest, -4.0, quarter, ALU.mult, ALU.add))
            link(dve.scalar_tensor_tensor(near[:, 1, P:2 * P], rest, BIG, near[:, 1, P:2 * P], ALU.mult, ALU.add))
            dve.wait_ge(gate_hi, 1)
            for c, row in ((0, 0), (4, 32)):
                ins = dve.tensor_tensor(wif_lo[:, :, row:row + 4], wif[:, :, c:c + 4], wif_hi[:, :, row:row + 4],
                                        ALU.subtract)
            ins.then_inc(gate_lo, 1)
            split_xt(0, range(KT))
            for u in range(2):
                split_unit(u, u)
            dve.wait_ge(cw_ps, 1)
            dve.tensor_copy(cw[:, :, :], bank[6][:, 0:40].rearrange("p (k c) -> p k c", c=5)).then_inc(cw_sb, 1)
            dve.wait_ge(gate_tr, 1)
            dve.wait_ge(gb_in, 32)
            fbias = gb[32:36, 0:1]
            link(dve.tensor_scalar(zf[:, :], bank[7][32:36, :], fbias, None, ALU.add))
            link(dve.tensor_copy(mrow[:, :], zf[:, :]))
            dve.scalar_tensor_tensor(zf[:, :], mrow[:, :], -1.0, mrow[:, :], ALU.mult, ALU.min)\
               .then_inc(gate_exp, 1)
            dve.wait_ge(gate_ln, 1)
            link(dve.scalar_tensor_tensor(zf[:, :], mrow[:, :], 0.0, ex[:, :], ALU.min, ALU.subtract))
            link(dve.memset(ex[:, :], 1.0))
            link(dve.tensor_tensor_scan(mrow[:, :], ex[:, :], zf[:, :], 0.0, ALU.mult, ALU.add))
            link(dve.scalar_tensor_tensor(rows[0:4, :], bank[7][0:4, :], gb[0:4, 0:1], mrow[:, :],
                                          ALU.add, ALU.subtract))
            link(dve.tensor_copy(zf[:, :], mrow[:, :]))
            link(dve.tensor_tensor_scan(mrow[:, :], rows[0:4, :], rows[0:4, :], 0.0, ALU.max, ALU.max))
            dve.scalar_tensor_tensor(rows[32:36, :], zf[:, :], -1.0, mrow[:, :], ALU.mult, ALU.subtract)\
               .then_inc(rows_ready, 1)

            with dve.Fori(0, 2) as j:
                for i in range(4):
                    st = 4 * (i % 2)
                    split_unit(8 * j + (2 * i + 2), 0)
                    if i < 2:
                        dsts = [(qk[:, ds(j, 1), i, b, :].rearrange("p a t -> p (a t)"), bank[st + b][:, :])
                                for b in (2, 3)]
                    elif i == 2:
                        dsts = [(v[:, ds(j, 1), b, :, 0:HD].rearrange("p a h e -> p (a h) e"),
                                 bank[st + b][:, :].rearrange("p (h e) -> p h e", e=HD)) for b in (2, 3)]
                    else:
                        dsts = [(og[:, ds(j, 1), b, :].rearrange("p a t -> p (a t)"), bank[st + b][:, :])
                                for b in (2, 3)]
                    evacuate(4 * j + i, dsts)
                    split_unit(8 * j + (2 * i + 3), 1)
            dve.wait_ge(mb_ps, 1)
            for i in (2, 3):
                ins = dve.tensor_copy(mb[:, i, :], bank[i][:, :])
            ins.then_inc(mb_sb, 1)
            dve.wait_ge(uc_ps, 1)
            dve.tensor_copy(uc[:, :, :], bank[4][:, 0:256].rearrange("p (t c) -> p t c", c=64)).then_inc(uc_sb, 1)

            def weigh(pair):
                for par in range(2):
                    n = 2 * pair + par
                    dve.wait_ge(s_ready, n + 1)
                    dve.wait_ge(d_ready, n + 1)
                    if pair >= 2:
                        dve.wait_ge(o_ready, n - 3)
                    b = 3 * par
                    src = (bank[b][:, :], bank[b + 1][:, 0:384], bank[b + 2][:, 0:256], bank[b + 1][:, 384:512])
                    for kb in range(NT):
                        w = T - P * kb
                        o = 0 if n < NH else OFF[kb]
                        ins = dve.tensor_tensor(pt[pair % 2][par][:, OFF[kb]:OFF[kb] + w], src[kb], dd[par][:, o:o + w],
                                                ALU.mult)
                    ins.then_inc(pt_ready, 1)

            def pair_stats(src_of):
                for c in range(8):
                    ins = dve.bn_stats(stat[:, c, :], src_of(c // NT, c % NT))
                link(ins)
                for c in range(8):
                    ins = dve.bn_aggr(mv[:, c, :], stat[:, c, :])
                link(ins)
                rsqrt(mv[:, :, 1], 8)

            def pair_normalise(pair, src_of):
                for par in range(2):
                    if pair:
                        dve.wait_ge(y_done, 2 * pair + par - 1)
                    for t in range(NT):
                        c = NT * par + t
                        ins = dve.tensor_scalar(hm[par][:, t, :], src_of(par, t), mv[:, c, 0:1], rstd[:, c:c + 1],
                                                ALU.subtract, ALU.mult)
                    ins.then_inc(yn_ready, 1)
                dve.wait_ge(yn_ready, 2 * pair + 2)

            def finish_retention(pair):
                def out_of(par, t):
                    return bank[6 + par][:, t * HD:(t + 1) * HD]

                dve.wait_ge(o_ready, 2 * pair + 2)
                pair_stats(out_of)
                pair_normalise(pair, out_of)
                dve.tensor_copy(nwt[:, 0:1], rstd[:, 0:1]).then_inc(o_read, 1)

            def finish_mlstm(pair):
                hd = 2 * pair - NH
                dve.wait_ge(o_ready, 2 * pair + 2)
                dve.wait_ge(y_done, 2 * pair)
                dve.wait_ge(en_sb, 1)
                for par in range(2):
                    dve.tensor_copy(nmr[:, NT * par:NT * par + 3],
                                    bank[6 + par][:, 0:3 * VW].rearrange("p (t c) -> p t c", c=VW)[:, :, HD])
                    ins = dve.tensor_copy(nmr[:, NT * par + 3:NT * par + 4], mlstm_out(par, 3)[:, HD:VW])
                link(ins)
                link(dve.scalar_tensor_tensor(nwt[:, :], nmr[:, :], -1.0, nmr[:, :], ALU.mult, ALU.max))
                link(dve.tensor_tensor(nwt[:, :].rearrange("p (h t) -> p h t", t=NT),
                                       nwt[:, :].rearrange("p (h t) -> p h t", t=NT),
                                       en[:, :, hd:hd + 2].rearrange("p t h -> p h t"), ALU.max))
                link(dve.reciprocal(nwt[:, :], nwt[:, :]))
                for par in range(2):
                    for t in range(NT):
                        c = NT * par + t
                        ins = dve.scalar_tensor_tensor(hm[par][:, t, :], mlstm_out(par, t)[:, 0:HD], nwt[:, c:c + 1],
                                                       og[:, 0, t, (hd + par) * HD:(hd + par + 1) * HD],
                                                       ALU.mult, ALU.mult)
                ins.then_inc(o_read, 1)
                dve.wait_ge(o_read, pair + 1)
                pair_stats(lambda par, t: hm[par][:, t, :])
                pair_normalise(pair, lambda par, t: hm[par][:, t, :])

            dve.wait_ge(w_lo, U_WOUT + 2 + 2)
            weigh(0)
            weigh(1)
            finish_retention(0)
            weigh(2)
            finish_retention(1)
            weigh(3)
            finish_mlstm(2)
            finish_mlstm(3)

            def tile_stats(t, s):
                return dve.bn_stats(stat[:, 2 * t + s, :], h[:, t, s * C:(s + 1) * C])

            def residual(chunk, units, st, half):
                dve.wait_ge(unit_done, units + 2)
                for t in range(NT):
                    hs = h[:, t, half * C:(half + 1) * C]
                    ins = dve.scalar_tensor_tensor(hs, hs, ALPHA, bank[st + t][:, :], ALU.mult, ALU.add)
                ins.then_inc(ev_d, 1)
                dve.wait_ge(ev_d, chunk + 1 + 2)
                for t in range(NT):
                    ins = tile_stats(t, half)
                link(ins)

            def layer_norm(n):
                for t in range(NT):
                    ins = dve.bn_aggr(mv[:, t, :], stat[:, 2 * t:2 * t + 2, :])
                link(ins)
                rsqrt(mv[:, 0:NT, 1], NT)
                dve.scalar_tensor_tensor(nmr[:, 0:NT], mv[:, 0:NT, 0], -1.0, rstd[:, 0:NT], ALU.mult, ALU.mult)\
                   .then_inc(ln_nmr, 1)
                dve.wait_ge(ln_in, 32 * (n + 1))
                for t in range(NT):
                    dve.wait_ge(ln_norm, 4 * n + t + 1)
                    ins = dve.tensor_tensor(h[:, t, :], h[:, t, :], lngb[:, 0, :], ALU.mult)
                    if t % 2 == 0:
                        ins.then_inc(ln_scaled, 1)
                    else:
                        link(ins)
                        dve.tensor_tensor(h[:, t, :], h[:, t, :], lngb[:, 1, :], ALU.add).then_inc(ln_out[1], 1)

            def picks(l, made, q):
                for par in range(2):
                    pair = ds(q + par, 1)
                    made(dve.tensor_tensor(pick0[:, :, :], aoh[:, 0:NT, :],
                                           eq[:, 0:NT, pair].to_broadcast([P, NT, P]), ALU.mult))
                    for t in range(NT):
                        ins = dve.scalar_tensor_tensor(pick[:, t, P * par:P * (par + 1)], aoh[:, NT + t, :],
                                                       eq[:, NT + t, pair], pick0[:, t, :], ALU.mult, ALU.add)
                    made(ins)
                dve.tensor_copy(nwt[:, 0:1], rstd[:, 0:1]).then_inc(pick_ready[l], 1)

            def route(l, made):
                row = lambda n: row128[:, 0:n]
                link(dve.memset(gs[:, :, :], -BIG))
                dve.wait_ge(aff_ready, l + 1)
                dve.wait_ge(rw_in, 32)
                link(dve.tensor_tensor(sel[:, :, :], aff[:, :, :], rb[:, None, :].to_broadcast([P, NT, E]), ALU.add))
                for t in range(NT):
                    for g in range(E // EG):
                        ins = dve.max(m8g[:, t, g, :], sel[:, t, EG * g:EG * (g + 1)])
                link(ins)
                link(dve.tensor_tensor(gs[:, :, 0:4], m8g[:, :, :, 0], m8g[:, :, :, 1], ALU.add))
                for t in range(NT):
                    ins = dve.max(gm[:, t, :], gs[:, t, :])
                link(ins)
                for t in range(NT):
                    ins = dve.max_index(gi[:, t, :], gm[:, t, :], gs[:, t, :])
                link(ins)
                link(dve.tensor_copy(gif[:, :], gi[:, :, 0]))
                link(dve.tensor_tensor(pen[:, :, :], row(4)[:, None, :].to_broadcast([P, NT, 4]),
                                       gif[:, :, None].to_broadcast([P, NT, 4]), ALU.is_equal))
                link(dve.tensor_scalar(pen[:, :, :], pen[:, :, :], 1.0, BIG, ALU.subtract, ALU.mult))
                link(dve.tensor_tensor(msel[:, :, :].rearrange("p t (g e) -> p t g e", e=EG),
                                       sel[:, :, :].rearrange("p t (g e) -> p t g e", e=EG),
                                       pen[:, :, :, None].to_broadcast([P, NT, 4, EG]), ALU.add))
                for t in range(NT):
                    ins = dve.max(v8[:, t, :], msel[:, t, :])
                link(ins)
                for t in range(NT):
                    ins = dve.max_index(i8[:, t, :], v8[:, t, :], msel[:, t, :])
                link(ins)
                link(dve.tensor_copy(ef[:, :, :], i8[:, :, 0:2].rearrange("p t c -> p c t")))
                for c in range(2):
                    ins = dve.tensor_tensor(oh[:, c, :, :], row(E)[:, None, :].to_broadcast([P, NT, E]),
                                            ef[:, c, :, None].to_broadcast([P, NT, E]), ALU.is_equal)
                link(ins)
                dve.tensor_tensor(ohs[:, :, :], oh[:, 0, :, :], oh[:, 1, :, :], ALU.add).then_inc(oh_ready, 1)
                for c in range(2):
                    ins = dve.tensor_tensor(t1[:, c, :, :], oh[:, c, :, :], aff[:, :, :], ALU.mult)
                link(ins)
                link(dve.tensor_reduce(ga[:, :, :], t1[:, :, :, :], AX.X, ALU.add))
                link(dve.tensor_tensor(gd[:, :], ga[:, 0, :], ga[:, 1, :], ALU.add))
                link(dve.reciprocal(gd[:, :], gd[:, :]))
                link(dve.tensor_tensor(ga[:, :, :], ga[:, :, :], gd[:, None, :].to_broadcast([P, 2, NT]), ALU.mult))
                dve.wait_ge(cnt_ps, l + 1)
                link(dve.tensor_tensor(cm[:, :, :], bank[5][:, P:P + E, None].to_broadcast([P, E, 8]),
                                       thr[:, None, :].to_broadcast([P, E, 8]), ALU.is_gt))
                link(dve.tensor_reduce(nb[:, :], cm[:, :, :], AX.X, ALU.add))
                link(dve.tensor_tensor_scan(bend[:, :], one[:, 0:1].to_broadcast([P, E]), nb[:, :], 0.0,
                                            ALU.mult, ALU.add))
                link(dve.tensor_tensor(bst[:, :], bend[:, :], nb[:, :], ALU.subtract))
                link(dve.tensor_scalar(bst[:, :], bst[:, :], float(B), None, ALU.mult))
                link(dve.tensor_tensor(pos[:, :, :], bank[5][:, 0:NT * E].rearrange("p (t e) -> p t e", e=E),
                                       bst[:, None, :].to_broadcast([P, NT, E]), ALU.add))
                for c in range(2):
                    ins = dve.tensor_tensor(t1[:, c, :, :], oh[:, c, :, :], pos[:, :, :], ALU.mult)
                link(ins)
                link(dve.tensor_reduce(dest[:, :], t1[:, :, :, :].rearrange("p c t e -> p (c t) e"), AX.X, ALU.add))
                link(dve.tensor_copy(di[:, :], dest[:, :]))
                link(dve.tensor_scalar(di[:, :], di[:, :], 7, None, ALU.arith_shift_right))
                link(dve.tensor_copy(pf[:, :], di[:, :]))
                link(dve.scalar_tensor_tensor(rm[:, :], pf[:, :], -float(P), dest[:, :], ALU.mult, ALU.add))
                link(dve.tensor_tensor(aoh[:, :, :], row(P)[:, None, :].to_broadcast([P, 8, P]),
                                       rm[:, :, None].to_broadcast([P, 8, P]), ALU.is_equal))
                link(dve.tensor_tensor(eq[:, :, :], row(NCOL)[:, None, :].to_broadcast([P, 8, NCOL]),
                                       pf[:, :, None].to_broadcast([P, 8, NCOL]), ALU.is_equal))
                picks(l, made, 0)
                for n, val in enumerate((dst_of, ga)):
                    ins = dve.tensor_tensor(
                        bv[:, :, n * NCOL:(n + 1) * NCOL], eq[:, :, :],
                        val[:, :, :].rearrange("p c t -> p (c t)")[:, :, None].to_broadcast([P, 8, NCOL]), ALU.mult)
                ins.then_inc(ab_ready, 1)
                link(dve.tensor_tensor(cmp[0:1, :, :], bend[0:1, None, :].to_broadcast([1, NBLK, E]),
                                       row(NBLK)[0:1, :, None].to_broadcast([1, NBLK, E]), ALU.is_le))
                link(dve.tensor_reduce(ber[0:1, :], cmp[0:1, :, :], AX.X, ALU.add))
                link(dve.tensor_scalar(be[0:1, :], ber[0:1, :], float(E - 1), None, ALU.min))
                link(dve.tensor_scalar(ni[0:1, 0:1], bend[0:1, E - 1:E], 3.0, None, ALU.add))
                link(dve.tensor_tensor(cmp[0:1, 0, 0:4], ber[0:1, 0:4], row(4)[0:1, :], ALU.not_equal))
                link(dve.tensor_reduce(ni[0:1, 2:3], cmp[0:1, 0, 0:4], AX.X, ALU.max))
                dve.tensor_scalar(ni[0:1, 1:2], ni[0:1, 0:1], 2, None, ALU.arith_shift_right).then_inc(blk_ready, 1)

            def experts(l, made):

                def keep_rows(n, half):
                    dve.wait_ge(xg_tr[l], 2 * n + (half + 1))
                    dve.tensor_copy(xgt[:, 4 * half + 2:4 * half + 4, :],
                                    bank[1][:, :].rearrange("p (k t) -> p k t", k=2)).then_inc(xgt_d[l], 1)

                def hidden(q, par):
                    dve.wait_ge(sg_ready[l], q + (par + 1))
                    dve.wait_ge(ht_tr[l], q + (par + 1))
                    dve.tensor_tensor(hh[par][:, :], sg[par][:, :], bank[2 + par][:, F:2 * F], ALU.mult)\
                       .then_inc(hh_ready[l], 1)

                def y_gated(q, par, it):
                    dve.wait_ge(dn_done[l], q + (par + 3))
                    dve.wait_ge(y_out[l][par], 16 * it + 16)
                    dve.tensor_scalar(yt[par][:, 512:D], bank[6][:, :], gt[:, ds(q + par, 1)], None, ALU.mult)\
                       .then_inc(yd_ready[l], 1)

                for half in range(2):
                    keep_rows(0, half)
                dve.wait_ge(tb_ps, l + 1)
                tb = bank[6]
                dve.tensor_scalar(td[:, :], tb[:, 0:NCOL], float(EMPTY), None, ALU.add)
                dve.tensor_copy(gt[:, :], tb[:, NCOL:2 * NCOL]).then_inc(tb_ready, 1)
                picks(l, made, 2)
                iters = dve.value_load(ni[0:1, 1:2], min_val=1, max_val=NBLK // 4)
                with dve.Fori(0, iters) as it, made.rolled(it, 4, 0):
                    q = 2 * it
                    hidden(q, 0)
                    hidden(q, 1)
                    keep_rows(it + 1, 0)
                    y_gated(q, 0, it)
                    keep_rows(it + 1, 1)
                    picks(l, made, q + 4)
                    y_gated(q, 1, it)

            def add_experts(l):
                for t in range(NT):
                    dve.wait_ge(y2_in[t], 16 * (l + 1))
                    link(dve.scalar_tensor_tensor(h[:, t, :], h[:, t, :], ALPHA, y2[t][:, 0:D], ALU.mult, ALU.add))
                    link(dve.tensor_tensor(h[:, t, :], h[:, t, :], y2[t][:, D:2 * D], ALU.add))
                    for s in range(2):
                        ins = tile_stats(t, s)
                link(ins)

            split_xt(8, range(KT))
            split_unit(U_WOUT + 2, 0)
            split_unit(U_WOUT + 3, 1)
            residual(8, U_WOUT + 2, 0, 0)
            residual(9, U_WOUT + 4, 4, 1)
            layer_norm(0)
            made = Order(dve, pick_o[0], link.count)
            route(0, made)
            experts(0, made)
            add_experts(0)
            layer_norm(1)

            for u in range(2):
                split_xt(16, range(4 * u, 4 * u + 4))
                split_unit(U_ODD + u, u)

            def odd_evac(c, st, dst, src_of, scale=None):
                evacuate(c, [(dst(b), src_of(bank[st + b][:, :])) for b in (2, 3)], scale)

            def q_scale(i):
                return None if i else DH ** -0.5

            for i, t in enumerate((q3, k3)):
                split_unit(U_ODD + 2 * i + 2, 0)
                odd_evac(10 + i, 4 * i, lambda b: t[:, 0, b, :], lambda s: s, q_scale(i))
                split_unit(U_ODD + 2 * i + 3, 1)
            with dve.Fori(1, 3) as g:
                for i, t in enumerate((q3, k3)):
                    split_unit(4 * g + (U_ODD + 2 * i + 2), 0)
                    odd_evac(2 * g + (10 + i), 4 * i,
                             lambda b: t[:, ds(g, 1), b, :].rearrange("p g (a j) -> p (g a) j", a=4),
                             perm, q_scale(i))
                    split_unit(4 * g + (U_ODD + 2 * i + 3), 1)
            for g in range(3):
                split_unit(U_ODDV + 2 * g + 2, 0)
                odd_evac(16 + g, 4 * (g % 2), lambda b: v3[:, g, b, :], lambda s: s)
                split_unit(U_ODDV + 2 * g + 3, 1)

            dve.wait_ge(unit_done, U_WOUT2 + 2)
            dve.memset(qz[0][64:P, :, :], 0.0)
            dve.memset(qz[1][0:64, :, :], 0.0)
            dve.wait_ge(ev_d, 19 + 2)
            dve.wait_ge(ev_a, 17 + 2)
            dve.tensor_copy(qz[0][0:64, :, :], q3[0:64, :, 0, :]).then_inc(qz_ready, 1)

            def biased(hp, k):
                lay, hd = k % 2, 2 * hp + k // 2
                if lay == 0:
                    dve.wait_ge(bh_ready, hd + 1)
                if isinstance(hp, int):
                    dve.wait_ge(s2_ready, 4 * hp + k + 3)
                else:
                    link.count.wait(s2_ready, 4 * hp + (k + 3), consts)
                for t in range(NT):
                    c = slice(P, 256) if (lay == 0 and t == 0) else slice(0, 256)
                    bk = bank[2 * lay + t // 2][:, 256 * (t % 2):256 * (t % 2) + 256]
                    ins = dve.tensor_tensor_reduce(out=sc[lay][:, t, c], in0=bk[:, c], in1=bh[k // 2 % 2][:, lay, c],
                                                   scale=1.0, scalar=-3.0e38, op0=ALU.add, op1=ALU.max,
                                                   accum_out=mm[lay][:, t:t + 1])
                link(ins)
                dve.tensor_scalar(nm[lay][:, :], mm[lay][:, :], -1.0, None, ALU.mult).then_inc(nm_ready, 1)
                dve.tensor_copy(ms[:, lay, :, ds(hd, 1)].rearrange("p t a -> p (t a)"), mm[lay][:, :])\
                   .then_inc(sb_ready, 1)

            def keep_weights(hp, k):
                dve.wait_ge(t_ready, 4 * hp + (k + 1))
                dve.wait_ge(o2_ready, 4 * hp + (k + 1))
                dve.tensor_copy(ptt[k % 2][:, 2:4, :].rearrange("p a c -> p (a c)"), bank[5][:, :])\
                   .then_inc(ptd, 1)

            def keep_out(hp, k):
                par, lay = k // 2, k % 2
                dve.wait_ge(o2_ready, 4 * hp + (k + 3))
                dve.wait_ge(qz_ready, 2 * hp + 2)
                dve.tensor_copy(
                    q3[:, lay, ds(hp, 1), :].rearrange("p g (t u c) -> p (g t) u c", t=NT, u=2)[:, :, par, :],
                    bank[6 + lay][:, 0:NT * DH].rearrange("p (t c) -> p t c", c=DH)).then_inc(oe_ready, 1)

            def pair_steps(hp, last):
                for k in range(4):
                    if not (last and k == 3):
                        biased(hp, k + 1)
                    keep_weights(hp, k)
                    if k:
                        keep_out(hp, k - 1)
                keep_out(hp, 3)

            biased(0, 0)
            with dve.Fori(0, 3) as hp, link.rolled(hp, 4, 3):
                pair_steps(hp, False)
            pair_steps(3, True)

            dve.wait_ge(far_in, 32)
            m1, d1, m2, d2 = ms[:, 0, :, :], dn[:, 0, :, :], me[:, :, 0:8], me[:, :, 8:16]
            dve.wait_ge(p_ready, 16)
            link(dve.tensor_tensor(mx[:, :, :], m1, m2, ALU.max))
            link(dve.tensor_tensor(w1[:, :, :], m1, mx[:, :, :], ALU.subtract))
            dve.tensor_tensor(w2[:, :, :], m2, mx[:, :, :], ALU.subtract).then_inc(mx_ready, 1)
            dve.wait_ge(we_ready, 1)
            link(dve.tensor_tensor(dsum[:, :, :], w1[:, :, :], d1, ALU.mult))
            link(dve.tensor_tensor(mx[:, :, :], w2[:, :, :], d2, ALU.mult))
            link(dve.tensor_tensor(dsum[:, :, :], dsum[:, :, :], mx[:, :, :], ALU.add))
            link(dve.reciprocal(dsum[:, :, :], dsum[:, :, :]))
            link(dve.tensor_tensor(w1[:, :, :], w1[:, :, :], dsum[:, :, :], ALU.mult))
            dve.tensor_tensor(w2[:, :, :], w2[:, :, :], dsum[:, :, :], ALU.mult).then_inc(wn_ready, 1)

            def near_out(hp):
                return q3[:, 0, hp, :].rearrange("p (t u c) -> p t u c", t=NT, u=2)

            for hp in range(4):
                ins = dve.tensor_tensor(near_out(hp), near_out(hp),
                                        w1[:, :, 2 * hp:2 * hp + 2, None].to_broadcast([P, NT, 2, DH]), ALU.mult)
            link(ins)
            for hp in range(4):
                dve.wait_ge(far_scaled, hp + 1)
                o2 = q3[:, 2, :, 2 * DH * hp:2 * DH * (hp + 1)].rearrange("p t (u c) -> p t u c", u=2)
                dve.tensor_tensor(near_out(hp), near_out(hp), o2, ALU.add).then_inc(yo_ready, 1)
            split_xt(24, range(4))
            residual(19, U_WOUT2 + 1, 4, 0)
            residual(20, U_WOUT2 + 2, 0, 1)
            layer_norm(2)
            made = Order(dve, pick_o[1], link.count)
            route(1, made)
            experts(1, made)
            add_experts(1)
            layer_norm(3)

        @block.tensor
        def _(pe):
            pe.sem_inc(unit_done, 2)
            pe.sem_inc(s2_ready, 2)
            pe.sem_inc(o2_ready, 2)
            for l in range(2):
                pe.sem_inc(gu_done[l], 2)
                pe.sem_inc(dn_done[l], 2)
                pe.sem_inc(ht_tr[l], 2)

            def keep_warm(n, b=7):
                for _ in range(n):
                    pe.matmul(bank[b][:, :], ident[:, :], dist[:, :], start=True, stop=True)

            def transpose_tiles(nk, src):
                for k in range(nk):
                    for t in range(NT):
                        ins = pe.transpose(bank[k][:, t * P:(t + 1) * P], src(k, t), ident[:, :])
                    ins.then_inc(xt_ps, 1)

            def unit(u, slot, half, out_of, x_cols=None, nk=8, xt_from=None):
                pe.wait_ge(w_lo, u + 3)
                if xt_from is not None:
                    pe.wait_ge(xt_l, xt_from + min(4 * (half + 1), nk))
                for i in range(4):
                    for kk in range(4):
                        k = 4 * half + kk
                        for n, (xp, wp) in enumerate(((xt_hi, wh), (xt_hi, wl), (xt_lo, wh))):
                            if x_cols is None:
                                a, b = wp[slot][:, kk, i * P:(i + 1) * P], xp[:, k, :]
                            else:
                                a, b = x_cols(xp, k, i), wp[slot][:, kk, :]
                            ins = pe.matmul(out_of(i), a, b, start=(k == 0 and n == 0),
                                            stop=(k == nk - 1 and n == 2))
                ins.then_inc(unit_done, 1)

            def in_order(xp, k, i):
                return xp[:, k, i * P:(i + 1) * P]

            def by_residue(xp, k, i):
                return perm(xp[:, k, :])[:, i, :]

            def chunk(c, a, u, st, x_cols=None, xt_from=None):
                pe.wait_ge(ev_d, c + 1)
                if a is not None:
                    pe.wait_ge(ev_a, a + 1)
                for half in range(2):
                    unit(u + half, half, half, lambda i: bank[st + i][:, :], x_cols, xt_from=xt_from)

            pe.wait_ge(consts, 1)
            pe.wait_ge(x_in, 16)
            transpose_tiles(KT, lambda k, t: h[:, t, k * P:(k + 1) * P])
            pe.wait_ge(cw_in, 32)
            pe.wait_ge(xt_l, KT)
            for k in range(8):
                ins = pe.transpose(bank[6][:, 5 * k:5 * k + 5], cwr[0:5, k * P:(k + 1) * P], ident[0:5, 0:5])
            ins.then_inc(cw_ps, 1)
            pe.wait_ge(gate_lo, 1)
            for k in range(KT):
                for n, (xp, wp) in enumerate(((xt_hi, wif_hi), (xt_hi, wif_lo), (xt_lo, wif_hi))):
                    ins = pe.matmul(bank[7][:, :], wp[:, k, :], xp[:, k, :], start=(k == 0 and n == 0),
                                    stop=(k == KT - 1 and n == 2))
            ins.then_inc(gate_tr, 1)

            with pe.Fori(0, 2) as j:
                chunk(4 * j, 4 * j, 8 * j, 0)
                pe.wait_ge(rows_ready, 1)
                pe.wait_ge(cw_sb, 1)
                chunk(4 * j + 1, 4 * j + 1, 8 * j + 2, 4)
                chunk(4 * j + 2, 4 * j + 2, 8 * j + 4, 0, in_order)
                chunk(4 * j + 3, 4 * j + 3, 8 * j + 6, 4, in_order)

            pe.wait_ge(ev_a, 7 + 2)
            pe.wait_ge(ev_d, 7 + 2)
            for i in range(NH):
                ins = pe.matmul(bank[i][:, :], sel4[0:4, i, :], mrow[0:4, :], start=True, stop=True)
            ins.then_inc(mb_ps, 1)
            pe.wait_ge(ev_a, 8 + 2)
            pe.wait_ge(ev_d, 8 + 2)
            for t in range(NT):
                ins = pe.transpose(bank[4][:, 64 * t:64 * t + 64], rows[:, t * P:(t + 1) * P], ident[0:64, 0:64])
            ins.then_inc(uc_ps, 1)
            pe.wait_ge(mb_sb, 2)
            pe.wait_ge(uc_sb, 1)

            def scores(pair):
                for par in range(2):
                    n = 2 * pair + par
                    pe.wait_ge(ks_ready, n + 1)
                    if pair:
                        pe.wait_ge(pt_ready, n - 1)
                    b = 3 * par
                    dst = (bank[b][:, :], bank[b + 1][:, 0:384], bank[b + 2][:, 0:256], bank[b + 1][:, 384:512])
                    for kb in range(NT):
                        ins = pe.matmul(dst[kb], ks[par][:, kb * P:(kb + 1) * P],
                                        qk[:, 1 - n // NH, 0, n % NH, kb * P:T], start=True, stop=True)
                    ins.then_inc(s_ready, 1)

            def mix(pair):
                for par in range(2):
                    n = 2 * pair + par
                    pe.wait_ge(pt_ready, n + (3 if pair == 2 else 1))
                    if pair:
                        pe.wait_ge(o_read, pair)
                    for t in range(NT):
                        if n < NH:
                            dst, width = bank[6 + par][:, t * HD:(t + 1) * HD], HD
                        else:
                            dst, width = mlstm_out(par, t), VW
                        for kb in range(t + 1):
                            c = OFF[kb] + (t - kb) * P
                            ins = pe.matmul(dst, pt[pair % 2][par][:, c:c + P], v[:, 1 - n // NH, kb, n % NH, 0:width],
                                            start=(kb == 0), stop=(kb == t))
                    ins.then_inc(o_ready, 1)

            scores(0)
            for pair in range(4):
                if pair < 3:
                    scores(pair + 1)
                mix(pair)

            pe.wait_ge(y_done, 8)
            pe.wait_ge(o_read, 4)
            transpose_tiles(KT, lambda k, t: og[:, k // 4, t, (k % 4) * HD:(k % 4 + 1) * HD])
            chunk(8, None, U_WOUT, 0, in_order, xt_from=KT)
            chunk(9, None, U_WOUT + 2, 4, in_order)

            def router(l):
                pe.wait_ge(rw_in, 32)

                def logits(t):
                    pe.wait_ge(rt_sb, NT * l + t + 1)
                    for k in range(KT):
                        ins = pe.matmul(bank[4][:, t * E:(t + 1) * E], ht[:, k, t * P:(t + 1) * P], rw[:, k, :],
                                        start=(k == 0), stop=(k == KT - 1))
                    return ins

                pe.wait_ge(ev_d, (20 if l else 9) + 2)
                keep_warm(12, 7 if l else 3)
                for t in range(NT):
                    wait_ln(pe, 2 * l, t)
                    if t >= 2:
                        pe.wait_ge(rt_sb, NT * l + t - 1)
                    for k in range(KT):
                        ins = pe.transpose(bank[2 * (t % 2) + k // 4][:, (k % 4) * P:(k % 4 + 1) * P],
                                           h[:, t, k * P:(k + 1) * P], ident[:, :])
                    ins.then_inc(rt_ps, 1)
                    if t:
                        logits(t - 1)
                logits(NT - 1).then_inc(lg_ps, 1)
                keep_warm(8)
                pe.wait_ge(oh_ready, l + 1)
                for t in range(NT):
                    for s in range(t + 1):
                        ins = pe.matmul(bank[5][:, t * E:(t + 1) * E], (before if s == t else ones_bf)[:, :],
                                        ohs[:, s, :], start=(s == 0), stop=(s == t))
                for s in range(NT):
                    ins = pe.matmul(bank[5][:, P:P + E], ones_bf[:, :], ohs[:, s, :],
                                    start=(s == 0), stop=(s == NT - 1))
                ins.then_inc(cnt_ps, 1)
            def experts(l):
                keep_warm(5)
                pe.wait_ge(lo_ready, NT * (l + 1))

                def rows(n, half):
                    pe.wait_ge(pick_ready[l], n + 1)
                    if not (isinstance(n, int) and half == 0):
                        pe.wait_ge(xgt_a[l], 2 * n + half)
                        pe.wait_ge(xgt_d[l], 2 * n + half)
                    for k in range(4):
                        for t in range(NT):
                            for i, part in enumerate((h_hi, h_lo)):
                                ins = pe.matmul(bank[k // 2][:, (k % 2) * 2 * P:(k % 2 + 1) * 2 * P],
                                                part[:, t, 4 * half + k:D:KT], pick[:, t, :],
                                                start=(t == 0 and i == 0), stop=(t == NT - 1 and i == 1))
                    ins.then_inc(xg_tr[l], 1)

                def gate_up(q, par, it):
                    pe.wait_ge(xgt_a[l], q + 2)
                    pe.wait_ge(xgt_d[l], q + 2)
                    pe.wait_ge(hh_ready[l], q + (par + 1))
                    pe.wait_ge(wgu_in[l][par], 64 * it + 64)
                    for k in range(KT):
                        for b in range(2):
                            ins = pe.matmul(bank[2 + par][B * b:B * (b + 1), :], xgt[:, k, P * par + B * b:P * par + B * (b + 1)],
                                            wgu[:, par, b, :, k, :], start=(k == 0), stop=(k == KT - 1))
                    ins.then_inc(gu_done[l], 1)

                def down(q, par, it):
                    pe.wait_ge(hh_ready[l], q + (par + 3))
                    for k in range(2):
                        ins = pe.transpose(bank[4][:, k * P:(k + 1) * P], hh[par][:, k:F:2], ident[:, :])
                    ins.then_inc(ht_tr[l], 1)
                    pe.wait_ge(tb_ready, l + 1)
                    pe.wait_ge(ht_sb[l], q + (par + 1))
                    pe.wait_ge(wd_in[l][par], 32 * it + 32)
                    pe.wait_ge(ya_ready[l], q + (par + 1))
                    pe.wait_ge(yd_ready[l], q + (par + 1))
                    for n in range(2):
                        for k in range(2):
                            for b in range(2):
                                ins = pe.matmul(bank[5 + n][B * b:B * (b + 1), :], htt[par][:, k, B * b:B * (b + 1)],
                                                wd[:, par, b, k, n * 512:(n + 1) * 512],
                                                start=(k == 0), stop=(k == 1))
                    ins.then_inc(dn_done[l], 1)

                for half in range(2):
                    rows(0, half)
                pe.wait_ge(ab_ready, l + 1)
                for c in range(8):
                    ins = pe.matmul(bank[6][:, 0:2 * NCOL], aoh[:, c, :], bv[:, c, :],
                                    start=(c == 0), stop=(c == 7))
                ins.then_inc(tb_ps, 1)
                pe.wait_ge(blk_ready, l + 1)
                iters = pe.value_load(ni[0:1, 1:2], min_val=1, max_val=NBLK // 4)
                pe.wait_ge(first_right, l + 1)
                with pe.Fori(0, iters) as it:
                    q = 2 * it
                    gate_up(q, 0, it)
                    gate_up(q, 1, it)
                    for par in range(2):
                        rows(it + 1, par)
                        down(q, par, it)

            router(0)
            experts(0)
            for t in (2, 3):
                wait_ln(pe, 1, t)
            pe.wait_ge(moe_done[0], 1)
            pe.wait_ge(ln_nmr, 2)
            keep_warm(0)
            transpose_tiles(KT, lambda k, t: h[:, t, k * P:(k + 1) * P])
            for i in range(2):
                chunk(10 + i, 8 + i, U_ODD + 2 * i, 4 * i, xt_from=2 * KT)
            with pe.Fori(1, 3) as g:
                for i in range(2):
                    chunk(2 * g + (10 + i), 2 * g + (8 + i), 4 * g + (U_ODD + 2 * i), 4 * i)
            for g in range(3):
                chunk(16 + g, 14 + g, U_ODDV + 2 * g, 4 * (g % 2), by_residue if g else in_order)
            pe.wait_ge(ev_a, 17 + 2)
            pe.wait_ge(ev_d, 19 + 2)

            def pair_tile(hp, g, cols):
                return k3[:, g, ds(hp, 1), cols].rearrange("p a t -> p (a t)")

            def odd_scores(hp, k):
                par, lay, pair = k // 2 % 2, k % 2, hp + k // 4
                pe.wait_ge(qz_ready, 2 * hp + (k // 2 + 1))
                for t in range(NT):
                    blk = slice(t * P, (t + 1) * P)
                    bk = bank[2 * lay + t // 2][:, 256 * (t % 2):256 * (t % 2) + 256]
                    if lay == 0 and t == 0:
                        ins = pe.matmul(bk[:, P:256], qz[par][:, 0, blk], pair_tile(pair, 0, blk),
                                        start=True, stop=True)
                    elif lay == 0:
                        ins = pe.matmul(bk, qz[par][:, 0, blk], pair_tile(pair, 0, slice((t - 1) * P, (t + 1) * P)),
                                        start=True, stop=True)
                    else:
                        for g in (1, 2):
                            ins = pe.matmul(bk[:, (g - 1) * P:g * P], qz[par][:, g, blk],
                                            pair_tile(pair, g, blk), start=True, stop=True)
                ins.then_inc(s2_ready, 1)

            def weights_t(hp, k):
                lay = k % 2
                pe.wait_ge(p_ready, 4 * hp + (k + 1))
                for t in range(NT):
                    for c in range(2):
                        if lay == 0 and t == 0 and c == 0:
                            continue
                        ins = pe.transpose(bank[4 + t // 2][:, 256 * (t % 2) + c * P:256 * (t % 2) + (c + 1) * P],
                                           sc[lay][:, t, c * P:(c + 1) * P], ident[:, :])
                ins.then_inc(t_ready, 1)

            def odd_mix(hp, k):
                par, lay = k // 2, k % 2
                pe.wait_ge(pta, 4 * hp + (k + 1))
                pe.wait_ge(ptd, 4 * hp + (k + 1))
                pe.wait_ge(oe_ready, 4 * hp + (k + 1))
                hv = lambda g, t: v3[:, g, t, ds((2 * hp + par) * DH, DH)]
                for t in range(NT):
                    o = bank[6 + lay][:, t * DH:(t + 1) * DH]
                    w = lambda c: ptt[lay][:, t, c * P:(c + 1) * P]
                    if lay == 0 and t == 0:
                        ins = pe.matmul(o, w(1), hv(0, 0), start=True, stop=True)
                    else:
                        g = (0, 0) if lay == 0 else (1, 2)
                        s = (t - 1, t) if lay == 0 else (t, t)
                        pe.matmul(o, w(0), hv(g[0], s[0]), start=True, stop=False)
                        ins = pe.matmul(o, w(1), hv(g[1], s[1]), start=False, stop=True)
                ins.then_inc(o2_ready, 1)

            def pair_steps(hp, last):
                for k in range(4):
                    weights_t(hp, k)
                    if not (last and k >= 2):
                        odd_scores(hp, k + 2)
                    odd_mix(hp, k)

            odd_scores(0, 0)
            odd_scores(0, 1)
            with pe.Fori(0, 3) as hp:
                pair_steps(hp, False)
            pair_steps(3, True)

            for hp in range(4):
                pe.wait_ge(yo_ready, hp + 1)
                for t in range(NT):
                    ins = pe.transpose(bank[hp][:, t * P:(t + 1) * P], q3[:, 0, hp, t * P:(t + 1) * P], ident[:, :])
                ins.then_inc(xt_ps, 1)
            pe.wait_ge(xt_l, 3 * KT + 4)
            for c in range(2):
                unit(U_WOUT2 + c, c, 0, lambda i: bank[4 * (1 - c) + i][:, :], in_order, nk=4)
            router(1)
            experts(1)


_INS = ["x", "w_in_even", "i_bias", "f_bias", "conv_w", "conv_b", "mlstm_norm_g", "ret_norm_g", "w_out_even",
        "w_in_odd", "w_out_odd", "router_w", "router_bias", "w_gate", "w_up", "w_down", "ln_g", "ln_b"]


def kernel(**inputs):
    import numpy as _np
    import concourse.bacc as _bacc
    from concourse import mybir as _mybir
    from concourse.bass_utils import run_bass_kernel_spmd as _run

    nc = _bacc.Bacc("TRN2", target_bir_lowering=False, num_devices=1)
    arrays, args = {}, []
    for name in _INS:
        a = _np.ascontiguousarray(inputs[name])
        arrays[f"in_{name}"] = a
        args.append(nc.dram_tensor(f"in_{name}", a.shape, _mybir.dt.from_np(a.dtype), kind="ExternalInput").ap())
    o = nc.dram_tensor("out", inputs["x"].shape, _mybir.dt.float32, kind="ExternalOutput").ap()
    trunk(nc, *args, o)
    r = _run(nc, [arrays], core_ids=[0])
    return r.results[0]["out"]
```
